# Optimizing a Trainium2 kernel written in Bass

```python
import math
import jax
import jax.numpy as jnp
from jax import lax
import numpy as np

D_MODEL = 1024
BATCH = 1
SEQ = 128
DEPTH = 2
DEC_BATCH = 1
DEC_SEQ = 512
PAST_LEN = 128

GRID_W = 64
HEAD_DIM = 64
A_HEADS = 8
A_KV_HEADS = 2
B_HEADS = 8
NA_ROWS = 8
NA_COLS = 16
Q_BLOCK = 128
ROPE_THETA = 10000.0
D_INNER = 2 * D_MODEL
SSD_HEAD_DIM = 64
SSD_HEADS = D_INNER // SSD_HEAD_DIM
SSD_GROUPS = 4
SSD_STATE = 128
SSD_CONV = 5
SSD_CHUNK = 128
D_FF = 2816
N_MOD = 9
N_ATTN_LAYERS = (DEPTH + 1) // 2
N_SSD_LAYERS = DEPTH // 2
EPS = 1e-6

A_Q = A_HEADS * HEAD_DIM
A_KV = A_KV_HEADS * HEAD_DIM
B_W = B_HEADS * HEAD_DIM
ATTN_IN = A_Q + 2 * A_KV + 3 * B_W
ATTN_OUT = A_Q + B_W
SSD_BC = SSD_GROUPS * SSD_STATE
SSD_CONV_DIM = D_INNER + 2 * SSD_BC
SSD_IN = D_INNER + SSD_CONV_DIM + 2 * SSD_HEADS

kernel_name = "hybrid_flow_gqa_natten_ssd_macaron"

def rmsnorm(x, g):
    xf = x.astype(jnp.float32)
    y = xf * lax.rsqrt(jnp.mean(xf * xf, axis=-1, keepdims=True) + EPS)
    return (y * g.astype(jnp.float32)).astype(x.dtype)

def swiglu(x, w_gate, w_up, w_down):
    return (jax.nn.silu(x @ w_gate) * (x @ w_up)) @ w_down

def rope_2d(x, n_tok):
    t = jnp.arange(n_tok, dtype=jnp.int32)
    half = HEAD_DIM // 2
    quarter = half // 2
    inv = 1.0 / (ROPE_THETA ** (jnp.arange(quarter, dtype=jnp.float32) / quarter))

    def rot(xh, pos):
        ang = pos.astype(jnp.float32)[:, None] * inv[None, :]
        cos = jnp.cos(ang)[None, :, None, :]
        sin = jnp.sin(ang)[None, :, None, :]
        x1 = xh[..., :quarter].astype(jnp.float32)
        x2 = xh[..., quarter:].astype(jnp.float32)
        return jnp.concatenate([x1 * cos - x2 * sin, x2 * cos + x1 * sin], axis=-1)

    out = jnp.concatenate([rot(x[..., :half], t // GRID_W), rot(x[..., half:], t % GRID_W)], axis=-1)
    return out.astype(x.dtype)

def block_attention(q, k, v):
    b, tq, h, d = q.shape
    hkv = k.shape[2]
    rep = h // hkv
    scale = d ** -0.5
    qb = q.reshape(b, tq // Q_BLOCK, Q_BLOCK, hkv, rep, d).transpose(1, 0, 2, 3, 4, 5)

    def one_block(q_blk):
        s = jnp.einsum('bqgrd,bkgd->bgrqk', q_blk, k, preferred_element_type=jnp.float32) * scale
        p = jax.nn.softmax(s, axis=-1)
        return jnp.einsum('bgrqk,bkgd->bqgrd', p.astype(v.dtype), v)

    o = lax.map(one_block, qb)
    return o.transpose(1, 0, 2, 3, 4, 5).reshape(b, tq, h * d)

def neighbourhood_attention(q, k, v, k_ctx, v_ctx, rpb):
    b, t, h, d = q.shape
    rows = t // GRID_W
    wr = min(NA_ROWS, rows)
    scale = d ** -0.5
    r = jnp.arange(rows)
    r0 = jnp.clip(r - wr // 2, 0, rows - wr)
    band_rows = r0[:, None] + jnp.arange(wr)[None, :]
    n_band = wr * GRID_W
    kg = k.reshape(b, rows, GRID_W, h, d)[:, band_rows].reshape(b, rows, n_band, h, d)
    vg = v.reshape(b, rows, GRID_W, h, d)[:, band_rows].reshape(b, rows, n_band, h, d)
    qg = q.reshape(b, rows, GRID_W, h, d)
    col = jnp.arange(GRID_W)
    c0 = jnp.clip(col - NA_COLS // 2, 0, GRID_W - NA_COLS)
    key_col = jnp.tile(col, wr)
    key_row = jnp.repeat(band_rows, GRID_W, axis=1)
    in_win = (key_col[None, :] >= c0[:, None]) & (key_col[None, :] < c0[:, None] + NA_COLS)
    dr = key_row - r[:, None] + (NA_ROWS - 1)
    dc = jnp.clip(key_col[None, :] - col[:, None] + (NA_COLS - 1), 0, 2 * NA_COLS - 2)
    bias = rpb.astype(jnp.float32)[:, dr[:, None, :], dc[None, :, :]]
    s_band = jnp.einsum('brqhd,brkhd->bhrqk', qg, kg, preferred_element_type=jnp.float32) * scale + bias[None]
    s_band = jnp.where(in_win[None, None, None], s_band, -jnp.inf)
    s_ctx = jnp.einsum('brqhd,bkhd->bhrqk', qg, k_ctx, preferred_element_type=jnp.float32) * scale
    p = jax.nn.softmax(jnp.concatenate([s_band, s_ctx], axis=-1), axis=-1).astype(v.dtype)
    o = (jnp.einsum('bhrqk,brkhd->brqhd', p[..., :n_band], vg)
         + jnp.einsum('bhrqk,bkhd->brqhd', p[..., n_band:], v_ctx))
    return o.reshape(b, t, h * d)

def attention_mixer(h, w_in, w_out, q_norm, k_norm, rpb, ctx):
    b, t, _ = h.shape
    proj = h @ w_in
    qa, ka, va, qb, kb, vb = jnp.split(
        proj, [A_Q, A_Q + A_KV, A_Q + 2 * A_KV, A_Q + 2 * A_KV + B_W, A_Q + 2 * A_KV + 2 * B_W], axis=-1)
    qa = rmsnorm(qa.reshape(b, t, A_HEADS, HEAD_DIM), q_norm)
    ka = rmsnorm(ka.reshape(b, t, A_KV_HEADS, HEAD_DIM), k_norm)
    va = va.reshape(b, t, A_KV_HEADS, HEAD_DIM)
    qb = qb.reshape(b, t, B_HEADS, HEAD_DIM)
    kb = kb.reshape(b, t, B_HEADS, HEAD_DIM)
    vb = vb.reshape(b, t, B_HEADS, HEAD_DIM)
    if ctx is None:
        oa = block_attention(qa, ka, va)
        ob = block_attention(qb, kb, vb)
        new = (ka, va, kb, vb)
    else:
        ka_c, va_c, kb_c, vb_c = ctx
        qa_r = rope_2d(qa, t)
        ka_r = rope_2d(ka, t)
        oa = block_attention(qa_r, jnp.concatenate([ka_r, ka_c], axis=1), jnp.concatenate([va, va_c], axis=1))
        ob = neighbourhood_attention(qb, kb, vb, kb_c, vb_c, rpb)
        new = None
    out = jnp.concatenate([oa, ob], axis=-1) @ w_out
    return out, new

def centred_depthwise_conv(x, w, bias):
    pad = SSD_CONV // 2
    y = lax.conv_general_dilated(
        x, w[:, None, :].astype(x.dtype), window_strides=(1,), padding=[(pad, pad)],
        dimension_numbers=('NWC', 'WIO', 'NWC'), feature_group_count=x.shape[-1])
    return y + bias

def ssd_scan(x, dt, a, bm, cm, s0):
    b, L, H, P = x.shape
    G, N = bm.shape[2], bm.shape[3]
    E = H // G
    nc = L // SSD_CHUNK
    f32 = jnp.float32
    xc = x.astype(f32).reshape(b, nc, SSD_CHUNK, G, E, P)
    dtc = dt.reshape(b, nc, SSD_CHUNK, G, E)
    bc = bm.astype(f32).reshape(b, nc, SSD_CHUNK, G, N)
    cc = cm.astype(f32).reshape(b, nc, SSD_CHUNK, G, N)
    cs = jnp.cumsum(dtc * a.astype(f32).reshape(G, E), axis=2)
    xdt = xc * dtc[..., None]
    tri = jnp.tril(jnp.ones((SSD_CHUNK, SSD_CHUNK), dtype=bool))[None, None, :, :, None, None]
    seg = cs[:, :, :, None] - cs[:, :, None, :]
    lmat = jnp.exp(jnp.where(tri, seg, -jnp.inf))
    cb = jnp.einsum('bclgn,bcsgn->bclsg', cc, bc)
    y_diag = jnp.einsum('bclsge,bcsgep->bclgep', cb[..., None] * lmat, xdt)
    decay_out = jnp.exp(cs[:, :, -1:] - cs)
    chunk_states = jnp.einsum('bclgn,bclge,bclgep->bcgepn', bc, decay_out, xdt)
    chunk_decay = jnp.exp(cs[:, :, -1])

    def step(s, inp):
        st, dec = inp
        return s * dec[..., None, None] + st, s

    s_last, s_prev = lax.scan(
        step, s0.astype(f32).reshape(b, G, E, P, N),
        (jnp.moveaxis(chunk_states, 1, 0), jnp.moveaxis(chunk_decay, 1, 0)))
    s_prev = jnp.moveaxis(s_prev, 0, 1)
    y_off = jnp.einsum('bclgn,bcgepn,bclge->bclgep', cc, s_prev, jnp.exp(cs))
    return (y_diag + y_off).reshape(b, L, H, P), s_last.reshape(b, H, P, N)

def ssd_mixer(h, w_in, conv_w, conv_b, dt_bias, a_log, d_skip, g_norm, w_out, init):
    b, L, _ = h.shape
    proj = h @ w_in
    z, xbc, dt_raw = jnp.split(proj, [D_INNER, D_INNER + SSD_CONV_DIM], axis=-1)
    xbc = jax.nn.silu(centred_depthwise_conv(xbc, conv_w, conv_b))
    xs, bm, cm = jnp.split(xbc, [D_INNER, D_INNER + SSD_BC], axis=-1)
    xs = xs.reshape(b, L, SSD_HEADS, SSD_HEAD_DIM)
    bm = bm.reshape(b, L, SSD_GROUPS, SSD_STATE)
    cm = cm.reshape(b, L, SSD_GROUPS, SSD_STATE)
    dt = jax.nn.softplus(dt_raw.astype(jnp.float32) + dt_bias.astype(jnp.float32))
    a = -jnp.exp(a_log.astype(jnp.float32))
    if init is None:
        s_f0 = jnp.zeros((b, SSD_HEADS, SSD_HEAD_DIM, SSD_STATE), jnp.float32)
        s_b0 = s_f0
    else:
        s_f0, s_b0 = init
    y_f, s_f = ssd_scan(xs, dt[..., :SSD_HEADS], a[0], bm, cm, s_f0)
    y_b, s_b = ssd_scan(xs[:, ::-1], dt[:, ::-1, SSD_HEADS:], a[1], bm[:, ::-1], cm[:, ::-1], s_b0)
    y = y_f + y_b[:, ::-1] + d_skip.astype(jnp.float32)[:, None] * xs.astype(jnp.float32)
    y = y.reshape(b, L, D_INNER) * jax.nn.silu(z.astype(jnp.float32))
    y = rmsnorm(y, g_norm).astype(h.dtype)
    return y @ w_out, (s_f, s_b)

def run_trunk(x, cond, ctx, p):
    is_ctx = ctx is None
    new_ak, new_av, new_nk, new_nv, new_sf, new_sb = [], [], [], [], [], []
    for l in range(DEPTH):
        mod = jax.nn.silu(cond) @ p['w_mod'][l] + p['b_mod'][l]
        sh1, sc1, g1, sh2, sc2, g2, sh3, sc3, g3 = jnp.split(mod[:, None, :], N_MOD, axis=-1)
        hf = rmsnorm(x, p['norm_pre'][l, 0]) * (1 + sc1) + sh1
        f = swiglu(hf, p['ffn_w_gate'][l, 0], p['ffn_w_up'][l, 0], p['ffn_w_down'][l, 0])
        x = x + 0.5 * g1 * rmsnorm(f, p['norm_post'][l, 0])
        hm = rmsnorm(x, p['norm_pre'][l, 1]) * (1 + sc2) + sh2
        j = l // 2
        if l % 2 == 0:
            layer_ctx = None if is_ctx else (ctx[0][:, j], ctx[1][:, j], ctx[2][:, j], ctx[3][:, j])
            o, new = attention_mixer(hm, p['attn_w_in'][j], p['attn_w_out'][j], p['attn_q_norm'][j],
                                     p['attn_k_norm'][j], p['na_rpb'][j], layer_ctx)
            if is_ctx:
                new_ak.append(new[0])
                new_av.append(new[1])
                new_nk.append(new[2])
                new_nv.append(new[3])
        else:
            init = None if is_ctx else (ctx[4][:, j], ctx[5][:, j])
            o, (s_f, s_b) = ssd_mixer(hm, p['ssd_w_in'][j], p['ssd_conv_w'][j], p['ssd_conv_b'][j],
                                      p['ssd_dt_bias'][j], p['ssd_a_log'][j], p['ssd_d'][j],
                                      p['ssd_norm'][j], p['ssd_w_out'][j], init)
            if is_ctx:
                new_sf.append(s_f)
                new_sb.append(s_b)
        x = x + g2 * rmsnorm(o, p['norm_post'][l, 1])
        hf = rmsnorm(x, p['norm_pre'][l, 2]) * (1 + sc3) + sh3
        f = swiglu(hf, p['ffn_w_gate'][l, 1], p['ffn_w_up'][l, 1], p['ffn_w_down'][l, 1])
        x = x + 0.5 * g3 * rmsnorm(f, p['norm_post'][l, 2])
    if is_ctx:
        return x, (jnp.stack(new_ak, axis=1), jnp.stack(new_av, axis=1), jnp.stack(new_nk, axis=1),
                   jnp.stack(new_nv, axis=1), jnp.stack(new_sf, axis=1), jnp.stack(new_sb, axis=1))
    return x, None

def setup_inputs(seed: int = 0) -> dict:
    key = jax.random.key(seed)
    ks = iter(jax.random.split(key, 40))

    def nrm(shape, scale):
        return scale * jax.random.normal(next(ks), shape, dtype=jnp.float32)

    NA, NS = N_ATTN_LAYERS, N_SSD_LAYERS
    x_prompt = nrm((BATCH, SEQ, D_MODEL), 1.0)
    x_sample = nrm((DEC_BATCH, DEC_SEQ, D_MODEL), 1.0)
    cache_attn_k = nrm((DEC_BATCH, NA, PAST_LEN, A_KV_HEADS, HEAD_DIM), 1.0)
    cache_attn_v = nrm((DEC_BATCH, NA, PAST_LEN, A_KV_HEADS, HEAD_DIM), 1.0)
    cache_na_k = nrm((DEC_BATCH, NA, PAST_LEN, B_HEADS, HEAD_DIM), 1.0)
    cache_na_v = nrm((DEC_BATCH, NA, PAST_LEN, B_HEADS, HEAD_DIM), 1.0)
    state_ssd_fwd = nrm((DEC_BATCH, NS, SSD_HEADS, SSD_HEAD_DIM, SSD_STATE), 0.5)
    state_ssd_bwd = nrm((DEC_BATCH, NS, SSD_HEADS, SSD_HEAD_DIM, SSD_STATE), 0.5)
    c = nrm((DEC_BATCH, D_MODEL), 1.0)
    c_ctx = nrm((D_MODEL,), 1.0)
    w_mod = nrm((DEPTH, D_MODEL, N_MOD * D_MODEL), 0.5 * D_MODEL ** -0.5)
    b_mod = nrm((DEPTH, N_MOD * D_MODEL), 0.02)
    norm_pre = 1.0 + nrm((DEPTH, 3, D_MODEL), 0.05)
    norm_post = 1.0 + nrm((DEPTH, 3, D_MODEL), 0.05)
    ffn_w_gate = nrm((DEPTH, 2, D_MODEL, D_FF), D_MODEL ** -0.5)
    ffn_w_up = nrm((DEPTH, 2, D_MODEL, D_FF), D_MODEL ** -0.5)
    ffn_w_down = nrm((DEPTH, 2, D_FF, D_MODEL), D_FF ** -0.5)
    attn_w_in = nrm((NA, D_MODEL, ATTN_IN), D_MODEL ** -0.5)
    attn_w_out = nrm((NA, ATTN_OUT, D_MODEL), ATTN_OUT ** -0.5)
    attn_q_norm = 1.0 + nrm((NA, HEAD_DIM), 0.05)
    attn_k_norm = 1.0 + nrm((NA, HEAD_DIM), 0.05)
    na_rpb = nrm((NA, B_HEADS, 2 * NA_ROWS - 1, 2 * NA_COLS - 1), 0.1)
    ssd_w_in = nrm((NS, D_MODEL, SSD_IN), D_MODEL ** -0.5)
    ssd_conv_w = nrm((NS, SSD_CONV, SSD_CONV_DIM), SSD_CONV ** -0.5)
    ssd_conv_b = nrm((NS, SSD_CONV_DIM), 0.02)
    dt0 = jnp.exp(jax.random.uniform(next(ks), (NS, 2 * SSD_HEADS), dtype=jnp.float32,
                                     minval=math.log(1e-3), maxval=math.log(1e-1)))
    ssd_dt_bias = jnp.log(jnp.expm1(dt0))
    ssd_a_log = jnp.log(jax.random.uniform(next(ks), (NS, 2, SSD_HEADS), dtype=jnp.float32,
                                           minval=1.0, maxval=16.0))
    ssd_d = 1.0 + nrm((NS, SSD_HEADS), 0.1)
    ssd_norm = 1.0 + nrm((NS, D_INNER), 0.05)
    ssd_w_out = nrm((NS, D_INNER, D_MODEL), D_INNER ** -0.5)
    return {
        'x_prompt': x_prompt, 'x_sample': x_sample,
        'cache_attn_k': cache_attn_k, 'cache_attn_v': cache_attn_v,
        'cache_na_k': cache_na_k, 'cache_na_v': cache_na_v,
        'state_ssd_fwd': state_ssd_fwd, 'state_ssd_bwd': state_ssd_bwd,
        'c': c, 'c_ctx': c_ctx,
        'w_mod': w_mod, 'b_mod': b_mod, 'norm_pre': norm_pre, 'norm_post': norm_post,
        'ffn_w_gate': ffn_w_gate, 'ffn_w_up': ffn_w_up, 'ffn_w_down': ffn_w_down,
        'attn_w_in': attn_w_in, 'attn_w_out': attn_w_out,
        'attn_q_norm': attn_q_norm, 'attn_k_norm': attn_k_norm, 'na_rpb': na_rpb,
        'ssd_w_in': ssd_w_in, 'ssd_conv_w': ssd_conv_w, 'ssd_conv_b': ssd_conv_b,
        'ssd_dt_bias': ssd_dt_bias, 'ssd_a_log': ssd_a_log, 'ssd_d': ssd_d,
        'ssd_norm': ssd_norm, 'ssd_w_out': ssd_w_out,
    }

def reference(x_prompt, x_sample, cache_attn_k, cache_attn_v, cache_na_k, cache_na_v,
              state_ssd_fwd, state_ssd_bwd, c, c_ctx,
              w_mod, b_mod, norm_pre, norm_post, ffn_w_gate, ffn_w_up, ffn_w_down,
              attn_w_in, attn_w_out, attn_q_norm, attn_k_norm, na_rpb,
              ssd_w_in, ssd_conv_w, ssd_conv_b, ssd_dt_bias, ssd_a_log, ssd_d, ssd_norm, ssd_w_out):
    p = {
        'w_mod': w_mod, 'b_mod': b_mod, 'norm_pre': norm_pre, 'norm_post': norm_post,
        'ffn_w_gate': ffn_w_gate, 'ffn_w_up': ffn_w_up, 'ffn_w_down': ffn_w_down,
        'attn_w_in': attn_w_in, 'attn_w_out': attn_w_out,
        'attn_q_norm': attn_q_norm, 'attn_k_norm': attn_k_norm, 'na_rpb': na_rpb,
        'ssd_w_in': ssd_w_in, 'ssd_conv_w': ssd_conv_w, 'ssd_conv_b': ssd_conv_b,
        'ssd_dt_bias': ssd_dt_bias, 'ssd_a_log': ssd_a_log, 'ssd_d': ssd_d,
        'ssd_norm': ssd_norm, 'ssd_w_out': ssd_w_out,
    }
    y_prompt, ctx_new = run_trunk(x_prompt, c_ctx[None, :], None, p)
    attn_k, attn_v, na_k, na_v, ssd_fwd, ssd_bwd = ctx_new
    y_sample, _ = run_trunk(x_sample, c,
                            (cache_attn_k, cache_attn_v, cache_na_k, cache_na_v, state_ssd_fwd, state_ssd_bwd), p)
    return (y_prompt, y_sample, attn_k, attn_v, na_k, na_v, ssd_fwd, ssd_bwd)


_drawn_inputs = setup_inputs


def setup_inputs(seed=0):
    import zlib

    import numpy as np

    out = dict(_drawn_inputs(seed))
    spreads = {}
    factors = {'attn_q_norm': 8.0, 'na_rpb': 7.557, 'ssd_d': 5.111, 'ssd_norm': 4.196}
    for name, (base, spread) in spreads.items():
        noise = np.random.default_rng([zlib.crc32(name.encode()), seed]).standard_normal(out[name].shape)
        drawn = base * np.exp(spread * noise) if base else spread * noise
        out[name] = jnp.asarray(drawn.astype(out[name].dtype))
    for name, factor in factors.items():
        out[name] = (out[name] * factor).astype(out[name].dtype)
    return out
```

```python
import concourse.bass as bass
from concourse import mybir
from contextlib import ExitStack
import numpy as np

F32 = mybir.dt.float32
F32R = mybir.dt.float32r
ACT = mybir.ActivationFunctionType
ALU = mybir.AluOpType
AXX = mybir.AxisListType.X

D = 1024
KD = D // 128
CTX, LAT = 128, 512
T = CTX + LAT
C = T // 2
FF = 2816
FFT = FF // 128
HALF = (12, 10)
KMAX = max(HALF)
EPS = 1e-6
NMOD = 9
MT = NMOD * KD
HEADS = 8
HD = 64
BLK = T // 128
SLOTS = 4
ZT, XT, BCT = 16, 16, 8


MODS = {0: (1, 1, 1, 0), 2: (1, 1, 1, 0), 3: (1, 0, 0, 0)}
FIRST_MODS = 16
AREA = 93184
NEG = -1e30


class Phase:

    def __init__(self, name, N, nk, q=0):
        self.name, self.N, self.nk, self.q = name, N, nk, q


def plan(subs):
    out, u, a, t = [], 0, 1, FIRST_MODS
    for s in subs:
        kind = s % 3
        if kind != 1:
            q1, q2, q3, q4 = MODS.get(s, (0, 0, 0, 0))
            ph = [Phase("guA", 2 * HALF[0], KD, q1), Phase("dnA", KD, HALF[0], q2),
                  Phase("guB", 2 * HALF[1], KD, q3), Phase("dnB", KD, HALF[1], q4)]
        elif s == 1:
            ph = [Phase("ain", 18, KD), Phase("aout", KD, KD)]
        else:
            ph = [Phase("sx", XT + BCT, KD), Phase("sz", ZT, KD), Phase("sdt", 1, KD),
                  Phase("soutA", KD, KD), Phase("soutB", KD, KD)]
        sub = {"s": s, "pre_a": a, "phases": ph}
        a += 1
        for p in ph:
            p.u0, p.a0, p.t0 = u, a, t
            f = 2 * (s // 3) + (s % 3) // 2
            p.w, p.w0 = {"guA": ("wgu", 2 * FFT * f), "guB": ("wgu", 2 * FFT * f + 2 * HALF[0]),
                         "dnA": ("wdA", KD * f), "dnB": ("wdB", KD * f)}.get(p.name, (p.name, 0))
            u, a, t = u + p.N, a + p.N, t + p.N * p.q
            if p.name == "ain":
                sub["va"], sub["qa"], sub["ra"] = a, a + 5, a + 10
                a += 15
            if p.name == "sdt":
                sub["ga"] = a
                a += 1
        sub["post_a"] = a
        a += 1
        out.append(sub)
    phases = [p for sub in out for p in sub["phases"]]
    for p, n in zip(phases, phases[1:] + [None]):
        p.next = n
    return out, t


def steps(eng, N, keep, body):
    rounds = (N - keep) // 4
    if rounds > 1:
        with eng.Fori(0, rounds) as r:
            for j in range(4):
                body(j, r)
    else:
        rounds = 0
    for n in range(4 * rounds, N):
        body(n, 0)


class Steps:

    def __init__(self, eng, sem):
        self.eng, self.sem, self.n, self.i = eng, sem, 0, 0

    def __call__(self, ins):
        ins.then_inc(self.sem, 1)
        self.n += 1

    def wait(self):
        self.eng.wait_ge(self.sem, self.n)


CHUNKS = [(4, False), (3, False), (2, False), (0, True), (1, True), (2, True), (3, True), (4, True)]
GROUPS, GH = 4, 8
ITEMS = [(c, j, g) for c, (j, second) in enumerate(CHUNKS) if second for g in range(GROUPS)]


def state_dirs(j, second):
    if j == 0:
        return (0, 1)
    return ((0,) if j < BLK - 1 else ()) if second else (1,)


STATES = [(c, j, g, w) for c, (j, second) in enumerate(CHUNKS) for g in range(GROUPS) for w in state_dirs(j, second)]


def attention_units():
    def heads(blocks):
        for t in range(4):
            for h in range(2):
                for b in blocks:
                    yield (t, h, b, 4, 64 * h, 0, t, None)
        for t in range(4):
            for h in range(2):
                for b in blocks:
                    yield (6 + t, h, b, 10 + t, 128 * (1 + t) + 64 * h, 1 + t, 4 + t, 2 * t + h if b else None)
    return [*heads([0]), *heads(range(1, BLK))]


def build(nc, d, subs):
    subplan, n_mod = plan(subs)
    phases = [p for sub in subplan for p in sub["phases"]]
    ctx = ExitStack()
    with ctx:
        def sb(name, shape, dt=F32):
            return ctx.enter_context(nc.sbuf_tensor(name, shape, dt))

        def sem(name):
            return ctx.enter_context(nc.semaphore(name))

        x = sb("x", [128, KD, T])
        M0 = (nc.sbuf_base + 31) // 32 * 32
        xh = sb("xh", [128, KD, T], F32R)
        xl = sb("xl", [128, KD, T], F32R)
        raw = sb("raw", [128, 2, KMAX * 128])
        wh = sb("wh", [128, 2, KMAX * 128], F32R)
        wl = sb("wl", [128, 2, KMAX * 128], F32R)
        rt = sb("rt", [128, T])
        rs = sb("rs", [128, T])
        mod = sb("mod", [128, 2 * MT, 2])
        bmod = sb("bmod", [128, 2 * MT, 2])
        npre = sb("npre", [128, 6, KD, 2])
        npost = sb("npost", [128, 6, KD, 2])
        ga = sb("ga", [128, KD, 2])
        gp = sb("gp", [128, KD, 2])
        cond = sb("cond", [128, KD, 2])
        scond = sb("scond", [128, KD, 2])
        ones = sb("ones", [128, 128])
        eps = sb("eps", [128, 1])
        tick = sb("tick", [128, 3])
        mraw = sb("mraw", [128, 2, KD * 128])
        A0 = (nc.sbuf_base + 31) // 32 * 32
        area = sb("area", [128, (AREA + 32) // 4])

        def at(name, shape, off, dt=F32):
            return nc.alloc_sbuf_tensor_at(name, shape, dt, offset=A0 + off)

        HB = KMAX * T * 4
        hh = at("hh", [128, KMAX, T], 0, F32R)
        hl = at("hl", [128, KMAX, T], HB, F32R)
        ft = at("ft", [128, KD, T], 2 * HB)
        sg = at("sg", [128, 2, T], 2 * HB + KD * T * 4)
        ht = at("ht", [128, T], 2 * HB + KD * T * 4 + 2 * T * 4)
        cst = sb("cst", [128, 3 * 128 + 64])
        gqk = sb("gqk", [128, 2])
        ident, hones, rotm, wmask = cst[:, 0:128], cst[:, 128:256], cst[:, 256:384], cst[:, 384:448]
        pt = at("pt", [128, 18, T], 0)
        kc = at("kc", [128, 5, 128], 46080)
        vc = at("vc", [128, 5 * 128], 48640)
        trig = at("trig", [128, 2, LAT], 51200)
        vt = at("vt", [128, BLK, 5 * 128], 55296)
        tb = at("tb", [128, 2, 14 * 64], 68096)
        pb = at("pb", [128, 3, T], 75264)
        ptr = at("ptr", [128, 2, T], 82944)
        sbias = at("sbias", [128, 2, T], 88064)
        def at_m(name, shape, off, dt=F32):
            return nc.alloc_sbuf_tensor_at(name, shape, dt, offset=M0 + off)

        xs = at("xs", [128, XT + BCT, T], 0)
        pad = at("pad", [128, 2, T + 8], 61440)
        zb = at("zb", [128, 2, T], 66624)
        xdt = at("xdt", [128, 2, 512], 61440)
        xw = at("xw", [128, 512], 65536)
        eb = at("eb", [128, 2, 512], 67584)
        cbt = at("cbt", [128, 2, 512], 71680)
        btok = at("btok", [128, 512], 75776)
        so = at("so", [128, 2, 512], 77824)
        tri = at("tri", [128, 4, 128], 81920)
        dtt = at("dtt", [128, BLK, 64], 83968)
        da = at("da", [128, BLK, 64], 85248)
        wdt = at("wdt", [128, 2, BLK, 32], 86528)
        cd = at("cd", [128, BLK, 64], 87808)
        dtr = at("dtr", [128, T], 89088)
        cw = at("cw", [128, 24, 6], 91648)
        svec = at("svec", [128, 2 * XT + 64 + 1], 92224)
        dvec, gvec, arow, dtb = svec[:, 0:XT], svec[:, XT:2 * XT], svec[:, 32:96], svec[:, 96:97]
        zin = at("zin", [128, 2, T], 87040)
        yh = at("yh", [128, KD, T], 40960, F32R)
        yl = at("yl", [128, KD, T], 0, F32R)
        sf = at_m("sf", [128, 2048], 0)
        sbw = at_m("sbw", [128, 2, 2048], 8192)
        rb = at_m("rb", [128, 2, 1024], 24576)
        em = at_m("em", [128, 2, 1024], 32768)
        xtok = mraw[:, :, :].rearrange("p a b -> p (a b)")
        st = sb("st", [128, 4, 4])
        P = ctx.enter_context(nc.psum_tensor("P", [128, 8, 512], F32))

        arrived = [sem("arrived0"), sem("arrived1")]
        m0arrived = [sem("m0arrived0"), sem("m0arrived1")]
        marrived = [sem("marrived0"), sem("marrived1")]
        in_sem = sem("in_sem")
        hi_done = sem("hi_done")
        lo_done = sem("lo_done")
        unit_done = sem("unit_done")
        acc_free = sem("acc_free")
        mod_used = sem("mod_used")
        consts = sem("consts")
        silu_c = sem("silu_c")
        own = sem("own")
        sg_done = sem("sg_done")
        hh_done = sem("hh_done")
        h_ready = sem("h_ready")
        sq_done = sem("sq_done")
        sq_used = sem("sq_used")
        rt_done = sem("rt_done")
        x_ready = sem("x_ready")
        t_done = sem("t_done")
        xh_done = sem("xh_done")
        xn_ready = sem("xn_ready")
        attn_in = sem("attn_in")
        tb_in = [sem("tb_in0"), sem("tb_in1")]
        kv_out = sem("kv_out")
        hq_sq = sem("hq_sq")
        hq_sum = sem("hq_sum")
        hq_root = sem("hq_root")
        hq_norm = sem("hq_norm")
        rot_done = sem("rot_done")
        roped = sem("roped")
        vtr_done = sem("vtr_done")
        qk_done = sem("qk_done")
        nm_done = sem("nm_done")
        p_done = sem("p_done")
        pn_done = sem("pn_done")
        tr_done = sem("tr_done")
        ptr_done = sem("ptr_done")
        pv_done = sem("pv_done")
        o_hi = sem("o_hi")
        o_done = sem("o_done")
        ssd_in = sem("ssd_in")
        st_in = sem("st_in")
        sb_spill = sem("sb_spill")
        sb_back = [sem("sb_back3"), sem("sb_back4")]
        st_out = [sem("st_out0"), sem("st_out1")]
        z_out = [sem("z_out0"), sem("z_out1")]
        z_back = [sem("z_back0"), sem("z_back1")]
        conv_step = sem("conv_step")
        conv_done = sem("conv_done")
        xs_done = sem("xs_done")
        z_done = sem("z_done")
        sp_dve = sem("sp_dve")
        sp_act = sem("sp_act")
        dt_tr = sem("dt_tr")
        da_done = sem("da_done")
        dec_sum = sem("dec_sum")
        dec_exp = sem("dec_exp")
        wdt_done = sem("wdt_done")
        prep_tr = sem("prep_tr")
        prep_cp = sem("prep_cp")
        cb_done = sem("cb_done")
        cbt_done = sem("cbt_done")
        rb_done = sem("rb_done")
        xdt_done = sem("xdt_done")
        xw_done = sem("xw_done")
        seg_done = sem("seg_done")
        e_done = sem("e_done")
        m_done = sem("m_done")
        off_done = sem("off_done")
        eb_done = sem("eb_done")
        offm_done = sem("offm_done")
        diag_done = sem("diag_done")
        s_sum = sem("s_sum")
        s_done = sem("s_done")
        y_done = sem("y_done")
        gated = sem("gated")
        g_sq = sem("g_sq")
        g_used = sem("g_used")
        g_root = sem("g_root")
        y_split = sem("y_split")
        out_sem = sem("out_sem")
        block = ctx.enter_context(nc.Block())

        def acc(a):
            s = 2 * (a % SLOTS)
            return P[:, s:s + 2, 0:C]

        def acc_mod(a, n):
            s = 2 * (a % SLOTS)
            return P[:, s + 1, C:C + 2 * n].rearrange("p (n c) -> p n c", c=2)

        def two(ap):
            return ap.rearrange("p (b c) -> p b c", b=2)

        def bc_last(ap, n):
            return ap.rearrange("p (a o) -> p a o", o=1).to_broadcast([ap.shape[0], ap.shape[1], n])

        def bc_mid(ap, n):
            return ap.rearrange("p (o b) -> p o b", o=1).to_broadcast([ap.shape[0], n, ap.shape[1]])

        def chunk(j):
            return slice(128 * j, 128 * j + 128)

        def flat(s):
            return P[:, 2 * s:2 * s + 2, :].rearrange("p b c -> p (b c)")

        def scores(g):
            return flat(g % 2)

        def one(buf, m, r):
            return buf[:, bass.ds(2 * r + m, 1), :].rearrange("p o t -> p (o t)")

        SIDES = ((0, 0, CTX), (1, CTX, T))

        @block.sync
        def _(sp):
            for dst, src in ((cond[:, :, :], d["cond"]), (bmod[:, :, :], d["bmod"]),
                             (npre[:, :, :, :], d["npre"]), (npost[:, :, :, :], d["npost"]),
                             (cst[:, :], d["cst"]), (x[:, :, :], d["x"])):
                sp.dma_start(dst, src).then_inc(in_sem, 16)

            for t in range(FIRST_MODS):
                if t >= 2:
                    sp.wait_ge(mod_used, t - 1)
                sp.dma_start(mraw[:, t % 2, :], d["wmod"][t]).then_inc(m0arrived[t % 2], 16)

            def unit_source(p, n, r):
                return d[p.w][bass.ds(4 * r + (p.w0 + n), 1), :, :].rearrange("o p n -> (o p) n")

            def load_unit(p, n, r):
                u = p.u0 + n
                if not (isinstance(r, int) and u < 2):
                    sp.wait_ge(lo_done, 4 * r + (u - 1))
                sp.dma_start(raw[:, u % 2, 0:p.nk * 128], unit_source(p, n, r)).then_inc(arrived[u % 2], 16)

            def attention_inputs(before):
                if before:
                    sp.wait_ge(unit_done, before)
                for dst, src in ((gqk[:, :], d["gqk"]), (kc[:, :, :], d["kc"]),
                                 (vc[:, :], d["vc"]), (trig[:, :, :], d["trig"])):
                    sp.dma_start(dst, src).then_inc(attn_in, 16)

            def ssd_inputs(idx):
                sp.wait_ge(xn_ready, 8 * (idx + 1))
                for dst, src in ((tri[:, :, :], d["tri"]), (cw[:, :, :], d["cw"]), (svec[:, :], d["svec"])):
                    sp.dma_start(dst, src).then_inc(ssd_in, 16)

            def ssd_states(p):
                sp.wait_ge(unit_done, p.u0)
                sp.dma_start(sf[:, :], d["s0"][0]).then_inc(st_in, 16)
                sp.dma_start(sbw[:, 0, :], d["s0"][1]).then_inc(st_in, 16)
                sp.wait_ge(s_done, GROUPS)
                sp.dma_start(d["spill"], sbw[:, 1, :]).then_inc(sb_spill, 16)
                n_ctx = sum(1 for c, *_ in STATES if c < 3)
                for i, (_, _, g, w) in enumerate([x for x in STATES if x[1] == 0]):
                    sp.wait_ge(s_done, n_ctx + i + 1)
                    sp.dma_start(d["s_ctx"][w][:, 512 * g:512 * g + 512], so[:, i % 2, :]).then_inc(st_out[i % 2], 16)
                sp.wait_ge(sb_spill, 16)
                sp.wait_ge(off_done, 2 * GROUPS)
                sp.dma_start(sbw[:, 1, :], d["spill"]).then_inc(sb_back[0], 16)
                sp.wait_ge(off_done, 4 * GROUPS)
                sp.dma_start(sbw[:, 0, :], d["s0"][1]).then_inc(sb_back[1], 16)
                sp.wait_ge(y_done, len(ITEMS))
                for f in range(ZT):
                    if f >= 2:
                        sp.wait_ge(gated, f - 1)
                    sp.wait_ge(z_out[f % 2], 16 * (ZT // 2))
                    sp.dma_start(zin[:, f % 2, :], d["zspill"][f]).then_inc(z_back[f % 2], 16)

            for p in phases:
                if p.name == "soutA":
                    load_unit(p, 0, 0)
                    load_unit(p, 1, 0)
                    ssd_states(p)
                    for n in range(2, p.N):
                        load_unit(p, n, 0)
                elif p.u0 == 0 or p.name in ("ain", "sx"):
                    for n in range(4):
                        load_unit(p, n, 0)
                        if n == 1 and p.name == "ain":
                            attention_inputs(p.u0)
                        if n == 1 and p.name == "sx":
                            ssd_inputs([sub["s"] for sub in subplan].index(4))
                    rounds = p.N // 4
                    with sp.Fori(1, rounds) as r:
                        for j in range(4):
                            load_unit(p, j, r)
                    for n in range(4 * rounds, p.N):
                        load_unit(p, n, 0)
                else:
                    steps(sp, p.N, 0, lambda n, r: load_unit(p, n, r))
            sp.wait_ge(x_ready, 8 * len(subplan))
            sp.dma_start(d["y"], x[:, :, :]).then_inc(out_sem, 16)
            sp.wait_ge(out_sem, 16)

        @block.gpsimd
        def _(pool):
            def load_mod(t, r):
                pool.dma_start(mraw[:, t, :], d["wmod"][bass.ds(2 * r + t, 1), :, :].rearrange("o p n -> (o p) n")
                               ).then_inc(marrived[t], 16)

            if n_mod > FIRST_MODS:
                with pool.Fori(FIRST_MODS // 2, n_mod // 2) as r:
                    for t in range(2):
                        pool.wait_ge(mod_used, 2 * r + (t - 1))
                        load_mod(t, r)

            if any(p.name == "sx" for p in phases):
                G = nc.gpsimd
                pool.wait_ge(ssd_in, 48)
                pool.wait_ge(da_done, 1)
                pool.wait_ge(wdt_done, 1)
                for b in range(2):
                    pool.wait_ge(z_out[b], 16 * (ZT // 2))

                def decay_operand(i):
                    c, j, g = ITEMS[i]
                    for w in range(2):
                        if i:
                            pool.wait_ge(seg_done, 2 * (i - 1) + w + 1)
                        G.tensor_tensor(rb[:, w, :].rearrange("p (h l) -> p h l", h=GH), bc_mid(tri[:, w, :], GH),
                                        bc_last(da[:, j, 32 * w + GH * g:32 * w + GH * g + GH], 128), ALU.mult).then_inc(rb_done, 1)

                def weighted(c, j, g, w):
                    n = STATES.index((c, j, g, w))
                    if n:
                        pool.wait_ge(s_sum, n)
                    G.tensor_tensor(xw[:, :].rearrange("p (h q) -> p h q", h=GH),
                                    xtok[:, 512 * g:512 * g + 512].rearrange("p (h q) -> p h q", h=GH),
                                    bc_last(wdt[:, w, j, GH * g:GH * g + GH], HD), ALU.mult).then_inc(xw_done, 1)

                for c, (j, second) in enumerate(CHUNKS):
                    if c == 2:
                        decay_operand(0)
                    pool.wait_ge(prep_cp, 5 * (c + 1))
                    for g in range(GROUPS):
                        if second:
                            i = ITEMS.index((c, j, g))
                            if i + 1 < len(ITEMS):
                                decay_operand(i + 1)
                            for w in range(2):
                                if i:
                                    pool.wait_ge(diag_done, i)
                                G.tensor_tensor(xdt[:, w, :].rearrange("p (h q) -> p h q", h=GH),
                                                xtok[:, 512 * g:512 * g + 512].rearrange("p (h q) -> p h q", h=GH),
                                                bc_last(dtt[:, j, 32 * w + GH * g:32 * w + GH * g + GH], HD),
                                                ALU.mult).then_inc(xdt_done, 1)
                        for w in state_dirs(j, second):
                            weighted(c, j, g, w)

        @block.scalar
        def _(act):
            act.wait_ge(in_sem, 16 * 6)
            nc.scalar.activation(scond[:, :, :], cond[:, :, :], ACT.Silu).then_inc(silu_c, 1)

            def high(p, n, r):
                u = p.u0 + n
                act.wait_ge(arrived[u % 2], r * 32 + 16 * (u // 2 + 1))
                nc.scalar.copy(wh[:, u % 2, 0:p.nk * 128], raw[:, u % 2, 0:p.nk * 128]).then_inc(hi_done, 1)

            def ahead(p, n, r):
                if n + 2 < p.N or not isinstance(r, int):
                    high(p, n + 2, r)
                elif p.next is not None:
                    k = n + 2 - p.N
                    high(*((p.next, k) if k < p.next.N else (p.next.next, k - p.next.N)), 0)

            def squares(src, idx, waits):
                for k in range(KD):
                    waits(k)
                    e = 8 * idx + k
                    if e >= 2:
                        act.wait_ge(sq_used, e - 1)
                    nc.scalar.square(sg[:, e % 2, :], src[:, k, :]).then_inc(sq_done, 1)

            def root(idx, a):
                act.wait_ge(sq_used, 8 * idx + 8)
                act.wait_ge(consts, 1)
                nc.scalar.activation(two(rt[:, :]), acc(a), ACT.Sqrt, bias=eps[:, 0:1], scale=1.0 / D).then_inc(rt_done, 1)

            units = attention_units()

            def load_bias(h):
                act.dma_start(tb[:, h % 2, :], d["bias"][h]).then_inc(tb_in[h % 2], 16)

            def attention(p, sub):
                act.wait_ge(attn_in, 16 * 4)
                for k in range(5):
                    act.wait_ge(acc_free, SLOTS + p.a0 + k + 1)
                    if k >= 2:
                        act.wait_ge(hq_sum, k - 1)
                    nc.scalar.square(pb[:, k % 2, :], pt[:, k, :]).then_inc(hq_sq, 1)
                    if k >= 1:
                        head_root(k - 1, sub)
                head_root(4, sub)
                act.wait_ge(hq_norm, 5)
                act.wait_ge(acc_free, SLOTS + p.a0 + p.N)
                act.dma_start(d["kv"][:, 0:2, :], pt[:, 4:6, 0:CTX]).then_inc(kv_out, 16)
                act.dma_start(d["kv"][:, 2:10, :], pt[:, 10:18, 0:CTX]).then_inc(kv_out, 16)
                load_bias(0)
                load_bias(1)
                for g in range(len(units) + 2):
                    if g < len(units):
                        b, bias = units[g][2], units[g][7]
                        n = T if b else CTX
                        act.wait_ge(nm_done, g + 1)
                        if g >= 3:
                            act.wait_ge(tr_done, g - 2)
                        if bias is None:
                            act.wait_ge(qk_done, g + 1)
                            src, scale = scores(g)[:, 0:n], HD ** -0.5
                        else:
                            src, scale = sbias[:, g % 2, :], 1.0
                        nc.scalar.activation(pb[:, g % 3, 0:n], src, ACT.Exp, bias=st[:, 1, g % 4:g % 4 + 1],
                                             scale=scale, accum_out=st[:, 2, g % 4:g % 4 + 1]).then_inc(p_done, 1)
                        if bias is not None and b == BLK - 1 and bias + 2 < HEADS:
                            load_bias(bias + 2)
                    if g >= 2:
                        h = g - 2
                        n = T if units[h][2] else CTX
                        act.wait_ge(tr_done, h + 1)
                        if h >= 2:
                            act.wait_ge(pv_done, h - 1)
                        nc.scalar.copy(ptr[:, h % 2, 0:n], flat(2)[:, 0:n]).then_inc(ptr_done, 1)

            def ssd(sub):
                A = nc.scalar.activation
                act.wait_ge(sp_dve, 1)
                A(em[0:64, 0, 0:T], rb[0:64, 0, 0:T], ACT.Exp).then_inc(sp_act, 1)
                act.wait_ge(sp_dve, 2)
                A(rb[0:64, 1, 0:T], em[0:64, 1, 0:T], ACT.Ln).then_inc(sp_act, 1)
                act.wait_ge(ssd_in, 48)
                A(arow, arow, ACT.Exp).then_inc(sp_act, 1)
                act.wait_ge(dec_sum, 1)
                nc.scalar.copy(rt[0:64, :], flat(0)[0:64, 0:T]).then_inc(dec_exp, 1)
                A(wdt[:, :, :, :], P[:, 2, 0:320].rearrange("p (w j h) -> p w j h", w=2, j=BLK), ACT.Exp).then_inc(dec_exp, 1)
                for b in range(2):
                    act.wait_ge(z_out[b], 16 * (ZT // 2))
                A(cd[:, :, :], P[:, 3, 0:320].rearrange("p (j h) -> p j h", j=BLK), ACT.Exp).then_inc(dec_exp, 1)

                def decays(i):
                    for w in range(2):
                        act.wait_ge(seg_done, 2 * i + w + 1)
                        if i:
                            act.wait_ge(diag_done, i)
                        A(em[:, w, :], P[:, 2 * w:2 * w + 2, :].rearrange("p b c -> p (b c)"), ACT.Exp).then_inc(e_done, 1)

                for c, (j, second) in enumerate(CHUNKS):
                    for k in range(5):
                        act.wait_ge(prep_tr, 5 * c + k + 1)
                        if c:
                            if k < 4:
                                act.wait_ge(xw_done, sum(1 for x in STATES if x[0] < c))
                                act.wait_ge(xdt_done, 2 * sum(1 for x in ITEMS if x[0] < c)) if c > 3 else None
                            else:
                                act.wait_ge(s_sum, sum(1 for x in STATES if x[0] < c))
                        dst = xtok[:, 512 * k:512 * k + 512] if k < 4 else btok[:, :]
                        nc.scalar.copy(dst, P[:, 6 + k % 2, :]).then_inc(prep_cp, 1)
                    if not second:
                        continue
                    for g in range(GROUPS):
                        i = ITEMS.index((c, j, g))
                        decays(i)
                        if j:
                            for w in range(2):
                                n = 2 * (i - GROUPS) + w
                                act.wait_ge(off_done, n + 1)
                                if i > GROUPS:
                                    act.wait_ge(y_done, i)
                                A(eb[:, w, :], P[:, 6, :], ACT.Exp).then_inc(eb_done, 1)
                for f in range(ZT):
                    act.wait_ge(gated, f + 1)
                    if f >= 2:
                        act.wait_ge(g_used, f - 1)
                    nc.scalar.square(sg[:, f % 2, :], xs[:, f, :]).then_inc(g_sq, 1)
                act.wait_ge(g_used, ZT)
                A(two(rt[:, :]), acc(sub["ga"]), ACT.Sqrt, bias=eps[:, 0:1], scale=1.0 / (128 * ZT)).then_inc(g_root, 1)

            def head_root(k, sub):
                act.wait_ge(hq_sum, k + 1)
                if k >= 2:
                    act.wait_ge(acc_free, SLOTS + sub["qa"] + k - 1)
                nc.scalar.activation(two(sbias[:, k % 2, :]), acc(sub["qa"] + k), ACT.Sqrt, bias=eps[:, 0:1],
                                     scale=1.0 / HD).then_inc(hq_root, 1)

            first = phases[0]
            high(first, 0, 0)
            high(first, 1, 0)
            for si, sub in enumerate(subplan):
                s = sub["s"]
                squares(x, 2 * si, lambda k: act.wait_ge(x_ready, 8 * (si - 1) + k + 1) if si else None)
                root(2 * si, sub["pre_a"])
                lay, j = s // 3, s % 3
                for k in range(KD):
                    act.wait_ge(t_done, 2 * (8 * si + k) + 2)
                    for c, t0, t1 in SIDES:
                        ins = nc.scalar.activation(xh[:, k, t0:t1], ft[:, k, t0:t1], ACT.Identity,
                                                   bias=mod[:, lay * MT + 3 * j * KD + k, c:c + 1])
                    ins.then_inc(xh_done, 1)
                for p in sub["phases"]:
                    if p.name in ("guA", "guB"):
                        def step(n, r):
                            act.wait_ge(unit_done, 4 * r + (p.u0 + n + 1))
                            ahead(p, n, r)
                            if n % 2 == 0:
                                nc.scalar.activation(two(sg[:, (n // 2) % 2, :]), acc(p.a0 + n), ACT.Silu
                                                     ).then_inc(sg_done, 1)
                        steps(act, p.N, 2, step)
                    elif p.name == "sx":
                        def step(n, r):
                            act.wait_ge(unit_done, 4 * r + (p.u0 + n + 1))
                            ahead(p, n, r)
                            act.wait_ge(conv_done, 4 * r + (n + 2))
                            nc.scalar.activation(one(xs, n, 2 * r), one(xs, n, 2 * r), ACT.Silu).then_inc(xs_done, 1)
                        steps(act, p.N, 2, step)
                    elif p.name == "sz":
                        for n in range(p.N):
                            act.wait_ge(unit_done, p.u0 + n + 1)
                            ahead(p, n, 0)
                            if n >= 2:
                                act.wait_ge(z_out[n % 2], 16 * (n // 2))
                            nc.scalar.activation(two(zb[:, n % 2, :]), acc(p.a0 + n), ACT.Silu).then_inc(z_done, 1)
                            act.wait_ge(z_done, n + 1)
                            act.dma_start(d["zspill"][n], zb[:, n % 2, :]).then_inc(z_out[n % 2], 16)
                    elif p.name == "sdt":
                        act.wait_ge(unit_done, p.u0 + 1)
                        high(p.next, 1, 0)
                        ssd(sub)
                    else:
                        def step(n, r):
                            act.wait_ge(unit_done, 4 * r + (p.u0 + n + 1))
                            ahead(p, n, r)
                        steps(act, p.N, 2, step)
                    if p.name == "ain":
                        attention(p, sub)
                dn = sub["phases"][-1]
                squares(ft, 2 * si + 1, lambda k: act.wait_ge(acc_free, SLOTS + dn.a0 + k + 1))
                root(2 * si + 1, sub["post_a"])

        @block.vector
        def _(dve):
            V = nc.vector
            me = Steps(dve, own)
            V.memset(ones[:, :], 1.0)
            V.memset(eps[:, :], EPS).then_inc(consts, 1)
            dve.wait_ge(consts, 1)
            V.memset(tick[:, 1:2], 0.0).then_inc(acc_free, SLOTS)
            V.memset(tick[:, 0:1], 0.0).then_inc(h_ready, 1)
            dve.wait_ge(in_sem, 16 * 6)

            def low(p, n, r):
                u = p.u0 + n
                dve.wait_ge(arrived[u % 2], r * 32 + 16 * (u // 2 + 1))
                dve.wait_ge(hi_done, 4 * r + (u + 1))
                V.tensor_tensor(wl[:, u % 2, 0:p.nk * 128], raw[:, u % 2, 0:p.nk * 128],
                                wh[:, u % 2, 0:p.nk * 128].bitcast(F32), ALU.subtract).then_inc(lo_done, 1)

            def ahead(p, n, r):
                if n + 2 < p.N or not isinstance(r, int):
                    low(p, n + 2, r)
                elif p.next is not None:
                    k = n + 2 - p.N
                    low(*((p.next, k) if k < p.next.N else (p.next.next, k - p.next.N)), 0)

            def take_mod(a, t, r4, n):
                V.tensor_tensor(mod[:, bass.ds(r4 + t, n), :], acc_mod(a, n), bmod[:, bass.ds(r4 + t, n), :], ALU.add)

            def reciprocal_of_root(idx):
                dve.wait_ge(rt_done, idx + 1)
                V.reciprocal(rs[:, :], rt[:, :]).then_inc(acc_free, 1)

            units = attention_units()

            def attention(p, sub):
                dve.wait_ge(attn_in, 16 * 4)
                for f in range(5):
                    dve.wait_ge(vtr_done, f + 1)
                    V.tensor_copy(vt[:, :, 128 * f:128 * f + 128],
                                  flat((sub["va"] + f) % SLOTS)[:, 0:T].rearrange("p (b c) -> p b c", b=BLK)).then_inc(acc_free, 1)
                dve.wait_ge(acc_free, SLOTS + p.a0 + p.N)
                for k in range(5):
                    dve.wait_ge(hq_root, k + 1)
                    if k:
                        dve.wait_ge(hq_norm, k)
                    V.reciprocal(rs[:, :], sbias[:, k % 2, :]).then_inc(acc_free, 1)
                    dve.wait_ge(acc_free, SLOTS + sub["qa"] + k + 1)
                    V.scalar_tensor_tensor(pt[:, k, :], pt[:, k, :], gqk[:, k // 4:k // 4 + 1], rs[:, :],
                                           ALU.mult, ALU.mult).then_inc(hq_norm, 1)
                for k in range(5):
                    dve.wait_ge(rot_done, k + 1)
                    if k == 0:
                        dve.wait_ge(hq_norm, 5)
                    V.tensor_tensor(ptr[:, 0, 0:LAT], flat((sub["ra"] + k) % SLOTS)[:, 0:LAT], trig[:, 1, :], ALU.mult).then_inc(acc_free, 1)
                    me(V.tensor_tensor(pt[:, k, CTX:T], pt[:, k, CTX:T], trig[:, 0, :], ALU.mult))
                    me.wait()
                    dve.wait_ge(acc_free, SLOTS + sub["ra"] + k + 1)
                    V.tensor_tensor(pt[:, k, CTX:T], pt[:, k, CTX:T], ptr[:, 0, 0:LAT], ALU.add).then_inc(roped, 1)
                    dve.wait_ge(roped, k + 1)
                for g in range(len(units) + 3):
                    if g < len(units):
                        front(g)
                    if 1 <= g <= len(units):
                        h = g - 1
                        n = T if units[h][2] else CTX
                        dve.wait_ge(p_done, h + 1)
                        me(V.reciprocal(st[:, 3, h % 4:h % 4 + 1], st[:, 2, h % 4:h % 4 + 1]))
                        me.wait()
                        V.tensor_scalar(pb[:, h % 3, 0:n], pb[:, h % 3, 0:n], st[:, 3, h % 4:h % 4 + 1], None,
                                        ALU.mult).then_inc(pn_done, 1)
                    if g >= 3:
                        h = g - 3
                        _, half, b, _, _, _, to, _ = units[h]
                        rows, cols = slice(64 * half, 64 * half + 64), slice(128 * b, 128 * b + 128)
                        dve.wait_ge(pv_done, h + 1)
                        V.tensor_copy(xh[rows, to, cols], P[rows, 6 + h % 2, 0:128]).then_inc(o_hi, 1)
                        dve.wait_ge(o_hi, h + 1)
                        V.tensor_tensor(xl[rows, to, cols], P[rows, 6 + h % 2, 0:128], xh[rows, to, cols].bitcast(F32),
                                        ALU.subtract).then_inc(o_done, 1)
                dve.wait_ge(kv_out, 32)

            def ssd(p, sub):
                v, m, e, u = dtr[0:64, :], rs[0:64, :], em[0:64, 0, 0:T], em[0:64, 1, 0:T]
                neg, ln = rb[0:64, 0, 0:T], rb[0:64, 1, 0:T]
                dve.wait_ge(acc_free, SLOTS + p.a0 + 1)
                me(V.tensor_scalar(m, v, 0.0, None, ALU.max))
                me(V.tensor_scalar(neg, v, -1.0, None, ALU.mult))
                me.wait()
                V.tensor_tensor(neg, neg, v, ALU.min).then_inc(sp_dve, 1)
                dve.wait_ge(sp_act, 1)
                V.tensor_scalar(u, e, 1.0, None, ALU.add).then_inc(sp_dve, 1)
                dve.wait_ge(sp_dve, 2)
                me(V.tensor_scalar(neg, u, -1.0, 1e-30, ALU.add, ALU.max))
                me.wait()
                me(V.tensor_scalar(v, neg, 1e-30, None, ALU.is_equal))
                me(V.reciprocal(neg, neg))
                me.wait()
                dve.wait_ge(sp_act, 2)
                me(V.tensor_tensor(neg, neg, ln, ALU.mult))
                me.wait()
                me(V.tensor_tensor(neg, neg, v, ALU.add))
                me.wait()
                me(V.tensor_tensor(neg, neg, e, ALU.mult))
                me.wait()
                me(V.tensor_tensor(v, neg, m, ALU.add))
                me.wait()
                V.memset(tick[:, 0:1], 0.0).then_inc(sp_dve, 1)
                dve.wait_ge(dt_tr, 1)
                me(V.tensor_copy(dtt[:, :, :], P[:, 7, 0:320].rearrange("p (j h) -> p j h", j=BLK)))
                me.wait()
                dve.wait_ge(sp_act, 3)
                V.scalar_tensor_tensor(da[:, :, :], dtt[:, :, :], -1.0, bc_mid(arow, BLK), ALU.mult, ALU.mult).then_inc(da_done, 1)
                dve.wait_ge(dec_exp, 3)
                for w in range(2):
                    ins = V.tensor_tensor(wdt[:, w, :, :], wdt[:, w, :, :], dtt[:, :, 32 * w:32 * w + 32], ALU.mult)
                ins.then_inc(wdt_done, 1)
                dve.wait_ge(st_in, 32)
                for b in range(2):
                    dve.wait_ge(z_out[b], 16 * (ZT // 2))

                def take_state(c, j, g, w):
                    n = STATES.index((c, j, g, w))
                    cols = slice(512 * g, 512 * g + 512)
                    heads = lambda ap: ap.rearrange("p (h q) -> p h q", h=GH)
                    dve.wait_ge(s_sum, n + 1)
                    if j == 0:
                        k = 2 * g + w
                        if k >= 2:
                            dve.wait_ge(st_out[k % 2], 16 * (k // 2))
                        V.tensor_copy(so[:, k % 2, :], P[:, 7, :]).then_inc(s_done, 1)
                        return
                    decay = bc_last(cd[:, j, 32 * w + GH * g:32 * w + GH * g + GH], HD)
                    if w == 0:
                        src = dst = sf[:, cols]
                    else:
                        src, dst = sbw[:, (4 - j) % 2, cols], sbw[:, (5 - j) % 2, cols]
                        if j == 2 and g == 0:
                            dve.wait_ge(sb_spill, 16)
                    me.wait()
                    dve.wait_ge(s_done, n) if n else None
                    me(V.tensor_tensor(heads(dst), heads(src), decay, ALU.mult))
                    me.wait()
                    V.tensor_tensor(dst, dst, P[:, 7, :], ALU.add).then_inc(s_done, 1)

                for c, (j, second) in enumerate(CHUNKS):
                    if not second:
                        for g in range(GROUPS):
                            take_state(c, j, g, 1)
                        continue
                    dve.wait_ge(cb_done, c - 2)
                    if ITEMS[0][0] != c:
                        dve.wait_ge(m_done, 2 * ITEMS.index((c, j, 0)))
                    for w in range(2):
                        V.tensor_tensor(cbt[:, w, :].rearrange("p (g l) -> p g l", g=GROUPS),
                                        P[:, 7, :].rearrange("p (g l) -> p g l", g=GROUPS),
                                        bc_mid(tri[:, w, :], GROUPS), ALU.mult).then_inc(cbt_done, 1)
                    dve.wait_ge(cbt_done, 2 * (c - 2))
                    for g in range(GROUPS):
                        i = ITEMS.index((c, j, g))
                        for w in range(2):
                            dve.wait_ge(e_done, 2 * i + w + 1)
                            m3 = em[:, w, :].rearrange("p (h l) -> p h l", h=GH)
                            V.tensor_tensor(m3, m3, bc_mid(cbt[:, w, 128 * g:128 * g + 128], GH), ALU.mult).then_inc(m_done, 1)
                        if j:
                            for w in range(2):
                                n = 2 * (i - GROUPS) + w
                                dve.wait_ge(eb_done, n + 1)
                                V.tensor_tensor(eb[:, w, :], eb[:, w, :], P[:, 5, :], ALU.mult).then_inc(offm_done, 1)
                        for w in state_dirs(j, second):
                            take_state(c, j, g, w)
                        y = xs[:, 4 * g:4 * g + 4, chunk(j)]
                        q4 = lambda ap: ap.rearrange("p (q l) -> p q l", q=4)
                        me(V.tensor_tensor(y, y, bc_last(dvec[:, 4 * g:4 * g + 4], 128), ALU.mult))
                        me.wait()
                        if j:
                            dve.wait_ge(offm_done, 2 * (i - GROUPS) + 2)
                            for w in range(2):
                                me(V.tensor_tensor(y, y, q4(eb[:, w, :]), ALU.add))
                                me.wait()
                        dve.wait_ge(diag_done, i + 1)
                        V.tensor_tensor(y, y, q4(P[:, 4, :]), ALU.add).then_inc(y_done, 1)
                        dve.wait_ge(y_done, i + 1)
                for f in range(ZT):
                    dve.wait_ge(z_back[f % 2], 16 * (f // 2 + 1))
                    V.tensor_tensor(xs[:, f, :], xs[:, f, :], zin[:, f % 2, :], ALU.mult).then_inc(gated, 1)
                dve.wait_ge(g_root, 1)
                V.reciprocal(rs[:, :], rt[:, :]).then_inc(acc_free, 1)
                dve.wait_ge(acc_free, SLOTS + sub["ga"] + 1)
                dve.wait_ge(gated, ZT)
                for f in range(ZT):
                    h, l = (xh, xl) if f < KD else (yh, yl)
                    me(V.scalar_tensor_tensor(xs[:, f, :], xs[:, f, :], gvec[:, f:f + 1], rs[:, :], ALU.mult, ALU.mult))
                    me.wait()
                    me(V.tensor_copy(h[:, f % KD, :], xs[:, f, :]))
                    me.wait()
                    V.tensor_tensor(l[:, f % KD, :], xs[:, f, :], h[:, f % KD, :].bitcast(F32), ALU.subtract).then_inc(y_split, 1)
                    dve.wait_ge(y_split, f + 1)

            def front(g):
                b, bias = units[g][2], units[g][7]
                n = T if b else CTX
                mx, nm = st[:, 0, g % 4:g % 4 + 1], st[:, 1, g % 4:g % 4 + 1]
                if bias is not None and b == 1:
                    dve.wait_ge(tb_in[bias % 2], 16 * (bias // 2 + 1))
                    slot = tb[:, bias % 2, :].rearrange("p (m c) -> p m c", c=64)
                    me(V.tensor_tensor(slot, slot, wmask.rearrange("p (o c) -> p o c", o=1).to_broadcast([128, 14, 64]), ALU.add))
                    me.wait()
                dve.wait_ge(qk_done, g + 1)
                if bias is None:
                    me(V.reduce_max(mx, scores(g)[:, 0:n], AXX))
                    me.wait()
                    V.tensor_scalar(nm, mx, -HD ** -0.5, None, ALU.mult).then_inc(nm_done, 1)
                else:
                    if g >= 2:
                        dve.wait_ge(p_done, g - 1)
                    m0 = 64 * (6 - 2 * (b - 1))
                    me(V.scalar_tensor_tensor(sbias[:, g % 2, 0:LAT], scores(g)[:, 0:LAT], HD ** -0.5,
                                              tb[:, bias % 2, m0:m0 + LAT], ALU.mult, ALU.add))
                    me(V.tensor_scalar(sbias[:, g % 2, LAT:T], scores(g)[:, LAT:T], HD ** -0.5, None, ALU.mult))
                    me.wait()
                    me(V.reduce_max(mx, sbias[:, g % 2, :], AXX))
                    me.wait()
                    V.tensor_scalar(nm, mx, -1.0, None, ALU.mult).then_inc(nm_done, 1)

            low(phases[0], 0, 0)
            low(phases[0], 1, 0)
            dve.wait_ge(mod_used, FIRST_MODS)
            me(V.tensor_tensor(mod[:, 0:FIRST_MODS, :], P[:, 0, 0:2 * FIRST_MODS].rearrange("p (n c) -> p n c", c=2), bmod[:, 0:FIRST_MODS, :], ALU.add))
            V.memset(tick[:, 2:3], 0.0).then_inc(acc_free, 1)
            for si, sub in enumerate(subplan):
                s = sub["s"]
                lay, j = s // 3, s % 3
                m0 = lay * MT + 3 * j * KD
                me.wait()
                me(V.scalar_tensor_tensor(ga[:, :, :], mod[:, m0 + KD:m0 + 2 * KD, :], 1.0, npre[:, s, :, :], ALU.add, ALU.mult))
                me.wait()
                reciprocal_of_root(2 * si)
                dve.wait_ge(acc_free, SLOTS + sub["pre_a"] + 1)
                if si:
                    dve.wait_ge(x_ready, 8 * si)

                def scaled(k):
                    for c, t0, t1 in SIDES:
                        V.scalar_tensor_tensor(ft[:, k, t0:t1], x[:, k, t0:t1], ga[:, k, c:c + 1], rs[:, t0:t1],
                                               ALU.mult, ALU.mult).then_inc(t_done, 1)

                def lows(k):
                    dve.wait_ge(xh_done, 8 * si + k + 1)
                    for c, t0, t1 in SIDES:
                        ins = V.scalar_tensor_tensor(xl[:, k, t0:t1], ft[:, k, t0:t1], mod[:, m0 + k, c:c + 1],
                                                     xh[:, k, t0:t1].bitcast(F32), ALU.add, ALU.subtract)
                    ins.then_inc(xn_ready, 1)

                for k in range(KD):
                    scaled(k)
                    if k >= 1:
                        dve.wait_ge(t_done, 2 * (8 * si + k))
                        lows(k - 1)
                dve.wait_ge(t_done, 2 * (8 * si + KD))
                lows(KD - 1)
                for p in sub["phases"]:
                    if p.name in ("guA", "guB"):
                        hm0 = sum(HALF) * sum(1 for q in subplan[:si] if q["s"] % 3 != 1) + (HALF[0] if p.name == "guB" else 0)

                        def step(n, r):
                            dve.wait_ge(unit_done, 4 * r + (p.u0 + n + 1))
                            ahead(p, n, r)
                            if n % 2:
                                m, a = n // 2, p.a0 + n
                                if p.q:
                                    take_mod(a, p.t0 + 2 * p.q * m, 4 * p.q * r, 2 * p.q)
                                dve.wait_ge(sg_done, 2 * r + (hm0 + m + 1))
                                dve.wait_ge(h_ready, 2 * r + (hm0 + m + 1))
                                V.tensor_tensor(two(ht[:, :]), acc(a), two(sg[:, m % 2, :]), ALU.mult).then_inc(acc_free, 2)
                                dve.wait_ge(acc_free, 4 * r + (SLOTS + a + 1))
                                V.tensor_copy(one(hh, m, r), ht[:, :]).then_inc(hh_done, 1)
                                dve.wait_ge(hh_done, 2 * r + (hm0 + m + 1))
                                V.tensor_tensor(one(hl, m, r), ht[:, :], one(hh, m, r).bitcast(F32),
                                                ALU.subtract).then_inc(h_ready, 1)
                        steps(dve, p.N, 2, step)
                    elif p.name == "sx":
                        dve.wait_ge(ssd_in, 48)
                        me(V.memset(pad[:, :, :], 0.0))
                        me.wait()
                        V.memset(tick[:, 1:2], 0.0).then_inc(conv_done, 1)

                        def step(n, r):
                            dve.wait_ge(unit_done, 4 * r + (p.u0 + n + 1))
                            ahead(p, n, r)
                            a, b = p.a0 + n, n % 2
                            dve.wait_ge(conv_done, 4 * r + (n + 1))
                            V.tensor_copy(pad[:, b, 2:2 + CTX], acc(a)[:, 0, 0:CTX])
                            V.tensor_copy(pad[:, b, CTX + 6:C + 6], acc(a)[:, 0, CTX:C])
                            V.tensor_copy(pad[:, b, C + 6:T + 6], acc(a)[:, 1, :]).then_inc(acc_free, 1)
                            dve.wait_ge(acc_free, 4 * r + (SLOTS + a + 1))
                            w = cw[:, bass.ds(4 * r + n, 1), :].rearrange("p o k -> p (o k)")
                            out = one(xs, n, 2 * r)
                            for k in range(5):
                                for t0, t1, o in ((0, CTX, 0), (CTX, T, 4)):
                                    src = pad[:, b, t0 + o + k:t1 + o + k]
                                    if k == 0:
                                        ins = V.tensor_scalar(out[:, t0:t1], src, w[:, 0:1], w[:, 5:6], ALU.mult, ALU.add)
                                    else:
                                        ins = V.scalar_tensor_tensor(out[:, t0:t1], src, w[:, k:k + 1], out[:, t0:t1], ALU.mult, ALU.add)
                                if k < 4:
                                    ins.then_inc(conv_step, 1)
                                    dve.wait_ge(conv_step, 16 * r + (4 * n + k + 1))
                            ins.then_inc(conv_done, 1)
                        steps(dve, p.N, 2, step)
                    elif p.name == "sz":
                        for n in range(p.N):
                            dve.wait_ge(unit_done, p.u0 + n + 1)
                            ahead(p, n, 0)
                            dve.wait_ge(z_done, n + 1)
                            dve.wait_ge(acc_free, SLOTS + p.a0 + n)
                            V.memset(tick[:, 2:3], 0.0).then_inc(acc_free, 1)
                    elif p.name == "sdt":
                        dve.wait_ge(unit_done, p.u0 + 1)
                        low(p.next, 1, 0)
                        V.tensor_scalar(two(dtr[:, :]), acc(p.a0), dtb, None, ALU.add).then_inc(acc_free, 1)
                        ssd(p, sub)
                    else:
                        def step(n, r):
                            dve.wait_ge(unit_done, 4 * r + (p.u0 + n + 1))
                            ahead(p, n, r)
                            a = p.a0 + n
                            if p.q:
                                take_mod(a, p.t0 + p.q * n, 4 * p.q * r, p.q)
                            dst = None if p.name == "ain" else two(one(ft, n, 2 * r))
                            if p.name == "ain":
                                V.tensor_copy(two(one(pt, n, 2 * r)), acc(a)).then_inc(acc_free, 1)
                            elif p.name in ("dnA", "aout", "soutA"):
                                V.tensor_copy(dst, acc(a)).then_inc(acc_free, 1)
                            else:
                                V.tensor_tensor(dst, dst, acc(a), ALU.add).then_inc(acc_free, 1)
                        steps(dve, p.N, 2, step)
                    if p.name == "ain":
                        attention(p, sub)
                dve.wait_ge(acc_free, SLOTS + sub["post_a"])
                me(V.scalar_tensor_tensor(gp[:, :, :], mod[:, m0 + 2 * KD:m0 + 3 * KD, :], 1.0 if j == 1 else 0.5, npost[:, s, :, :], ALU.mult, ALU.mult))
                me.wait()
                reciprocal_of_root(2 * si + 1)
                dve.wait_ge(acc_free, SLOTS + sub["post_a"] + 1)

                def update(k):
                    me.wait()
                    V.tensor_tensor(x[:, k, :], x[:, k, :], ft[:, k, :], ALU.add).then_inc(x_ready, 1)

                for k in range(KD):
                    for c, t0, t1 in SIDES:
                        me(V.scalar_tensor_tensor(ft[:, k, t0:t1], ft[:, k, t0:t1], gp[:, k, c:c + 1], rs[:, t0:t1],
                                                  ALU.mult, ALU.mult))
                    update(k)

        @block.tensor
        def _(pe):
            pe.wait_ge(silu_c, 1)
            pe.wait_ge(in_sem, 16 * 6)
            pe.wait_ge(consts, 1)

            def mod_tile(t, r, q, out):
                if t < FIRST_MODS:
                    pe.wait_ge(m0arrived[t % 2], 16 * (t // 2 + 1))
                else:
                    pe.wait_ge(marrived[t % 2], r * (32 * q) + 16 * ((t - FIRST_MODS) // 2 + 1))
                for kk in range(KD):
                    ins = nc.tensor.matmul(out, mraw[:, t % 2, kk * 128:(kk + 1) * 128], scond[:, kk, :],
                                           start=(kk == 0), stop=(kk == KD - 1))
                ins.then_inc(mod_used, 1)

            pe.wait_ge(acc_free, SLOTS)
            for t in range(FIRST_MODS):
                mod_tile(t, 0, 0, P[:, 0, 2 * t:2 * t + 2])

            def norm_sum(idx, a):
                pe.wait_ge(acc_free, a + 1)
                for k in range(KD):
                    e = 8 * idx + k
                    pe.wait_ge(sq_done, e + 1)
                    for b in range(2):
                        ins = nc.tensor.matmul(acc(a)[:, b, :], ones[:, :], sg[:, e % 2, b * C:(b + 1) * C],
                                               start=(k == 0), stop=(k == KD - 1))
                    ins.then_inc(sq_used, 1)

            def unit(p, n, r, rh, rl):
                u, a = p.u0 + n, p.a0 + n
                pe.wait_ge(acc_free, 4 * r + (a + 1))
                gu = p.name[:2] == "gu"
                q = (2 * p.q * (n % 2) if gu else p.q)
                t0 = p.t0 + (n * p.q if not gu else (n - 1) * p.q)
                for j in range(q):
                    mod_tile(t0 + j, r, p.q, acc_mod(a, q)[:, j, :])
                pe.wait_ge(lo_done, 4 * r + (u + 1))
                s = u % 2
                for k in range(p.nk):
                    for w, m in ((wh, rh), (wh, rl), (wl, rh)):
                        for b in range(2):
                            ins = nc.tensor.matmul(acc(a)[:, b, :], w[:, s, k * 128:(k + 1) * 128],
                                                   m[:, k, b * C:(b + 1) * C],
                                                   start=(k == 0 and w is wh and m is rh),
                                                   stop=(k == p.nk - 1 and w is wl))
                ins.then_inc(unit_done, 1)

            units = attention_units()

            def attention(p, sub):
                pe.wait_ge(attn_in, 16 * 4)
                for f in range(5):
                    a, src = sub["va"] + f, 5 if f == 0 else 13 + f
                    pe.wait_ge(acc_free, max(a + 1, SLOTS + p.a0 + src + 1))
                    for b in range(BLK):
                        ins = nc.tensor.transpose(flat(a % SLOTS)[:, 128 * b:128 * b + 128], pt[:, src, 128 * b:128 * b + 128], ident)
                    ins.then_inc(vtr_done, 1)
                for k in range(5):
                    a = sub["qa"] + k
                    pe.wait_ge(acc_free, a + 1)
                    pe.wait_ge(hq_sq, k + 1)
                    for b in range(2):
                        ins = nc.tensor.matmul(acc(a)[:, b, :], hones, pb[:, k % 2, b * C:(b + 1) * C], start=True, stop=True)
                    ins.then_inc(hq_sum, 1)
                for k in range(5):
                    a = sub["ra"] + k
                    pe.wait_ge(acc_free, a + 1)
                    pe.wait_ge(hq_norm, k + 1)
                    nc.tensor.matmul(flat(a % SLOTS)[:, 0:LAT], rotm, pt[:, k, CTX:T], start=True, stop=True).then_inc(rot_done, 1)
                pe.wait_ge(acc_free, SLOTS + sub["ra"] + 5)
                pe.wait_ge(roped, 5)
                for g in range(len(units) + 3):
                    if g < len(units):
                        tq, half, b, tk, _, tc, _, _ = units[g]
                        rows = slice(64 * half, 64 * half + 64)
                        q = pt[rows, tq, 128 * b:128 * b + 128]
                        if g >= 2:
                            pe.wait_ge(p_done, g - 1)
                        if b:
                            nc.tensor.matmul(scores(g)[:, 0:LAT], q, pt[rows, tk, CTX:T], start=True, stop=True)
                            ins = nc.tensor.matmul(scores(g)[:, LAT:T], q, kc[rows, tc, :], start=True, stop=True)
                        else:
                            ins = nc.tensor.matmul(scores(g)[:, 0:CTX], q, pt[rows, tk, 0:CTX], start=True, stop=True)
                        ins.then_inc(qk_done, 1)
                    if 2 <= g < len(units) + 2:
                        h = g - 2
                        pe.wait_ge(pn_done, h + 1)
                        if h >= 1:
                            pe.wait_ge(ptr_done, h)
                        for j in range(BLK if units[h][2] else 1):
                            ins = nc.tensor.transpose(flat(2)[:, 128 * j:128 * j + 128], pb[:, h % 3, 128 * j:128 * j + 128], ident)
                        ins.then_inc(tr_done, 1)
                    if g >= 3:
                        h = g - 3
                        _, half, b, _, cv, _, _, _ = units[h]
                        out = P[64 * half:64 * half + 64, 6 + h % 2, 0:128]
                        pe.wait_ge(ptr_done, h + 1)
                        if h >= 2:
                            pe.wait_ge(o_done, h - 1)
                        vs = [vt[:, 1 + j, cv:cv + 64] for j in range(BLK - 1)] + [vc[:, cv:cv + 64]] if b else [vt[:, 0, cv:cv + 64]]
                        for j, v in enumerate(vs):
                            ins = nc.tensor.matmul(out, v, ptr[:, h % 2, 128 * j:128 * j + 128], start=(j == 0), stop=(j == len(vs) - 1))
                        ins.then_inc(pv_done, 1)
                pe.wait_ge(o_done, len(units))

            def ssd(p, sub):
                mm = nc.tensor.matmul
                pe.wait_ge(ssd_in, 48)
                pe.wait_ge(acc_free, SLOTS + p.a0 + 1)
                pe.wait_ge(sp_dve, 3)
                for j in range(BLK):
                    ins = nc.tensor.transpose(P[:, 7, 64 * j:64 * j + 64], dtr[0:64, chunk(j)], ident[0:64, 0:64])
                ins.then_inc(dt_tr, 1)
                pe.wait_ge(da_done, 1)
                for j in range(BLK):
                    for w in range(2):
                        mm(flat(0)[32 * w:32 * w + 32, chunk(j)], da[:, j, 32 * w:32 * w + 32], tri[:, w, :], start=True, stop=True)
                for w in range(2):
                    mm(P[:, 2, 160 * w:160 * w + 160].rearrange("p (j h) -> p j h", j=BLK), tri[:, 2 + w, :],
                       da[:, :, 32 * w:32 * w + 32], start=True, stop=True)
                mm(P[:, 3, 0:320], ones[:, :], da[:, :, :].rearrange("p j h -> p (j h)"), start=True, stop=True).then_inc(dec_sum, 1)
                pe.wait_ge(xs_done, XT + BCT)
                pe.wait_ge(dec_exp, 3)
                pe.wait_ge(st_in, 32)

                def decay_sums(i, w):
                    pe.wait_ge(rb_done, 2 * i + w + 1)
                    if i:
                        pe.wait_ge(e_done, 2 * (i - 1) + w + 1)
                    for b in range(2):
                        ins = mm(P[:, 2 * w + b, :], tri[:, 2 + w, :], rb[:, w, 512 * b:512 * b + 512], start=True, stop=True)
                    ins.then_inc(seg_done, 1)

                def chunk_state(c, j, g, w):
                    n = STATES.index((c, j, g, w))
                    pe.wait_ge(xw_done, n + 1)
                    if n:
                        pe.wait_ge(s_done, n)
                    mm(P[:, 7, :], btok[:, 128 * g:128 * g + 128], xw[:, :], start=True, stop=True).then_inc(s_sum, 1)

                for c, (j, second) in enumerate(CHUNKS):
                    for k in range(5):
                        if k >= 2:
                            pe.wait_ge(prep_cp, 5 * c + k - 1)
                        elif c:
                            pe.wait_ge(s_done, sum(1 for x in STATES if x[0] < c))
                            off = 2 * GROUPS * max(0, c - 4)
                            if off:
                                pe.wait_ge(eb_done, off)
                        for q in range(4):
                            ins = nc.tensor.transpose(P[:, 6 + k % 2, 128 * q:128 * q + 128], xs[:, 4 * k + q, chunk(j)], ident)
                        ins.then_inc(prep_tr, 1)
                    pe.wait_ge(prep_cp, 5 * c + 5)
                    if not second:
                        for g in range(GROUPS):
                            chunk_state(c, j, g, 1)
                        if c == 2:
                            decay_sums(0, 0)
                            decay_sums(0, 1)
                            pe.wait_ge(s_done, 3 * GROUPS)
                        continue
                    for g in range(GROUPS):
                        ins = mm(P[:, 7, 128 * g:128 * g + 128], xs[:, XT + g, chunk(j)], xs[:, XT + 4 + g, chunk(j)], start=True, stop=True)
                    ins.then_inc(cb_done, 1)
                    pe.wait_ge(cbt_done, 2 * (c - 2))
                    for g in range(GROUPS):
                        i = ITEMS.index((c, j, g))
                        for w in range(2):
                            if j:
                                n = 2 * (i - GROUPS) + w
                                if n:
                                    pe.wait_ge(offm_done, n)
                                S = sf if w == 0 else sbw[:, j % 2, :]
                                if w and j >= 3:
                                    pe.wait_ge(sb_back[j - 3], 16)
                                for q in range(4):
                                    t = 4 * g + q
                                    mm(P[:, 5, 128 * q:128 * q + 128], S[:, 128 * t:128 * t + 128], xs[:, XT + 4 + g, chunk(j)], start=True, stop=True)
                                for h in range(GH):
                                    k = 32 * w + GH * g + h
                                    ins = mm(P[64 * (h % 2):64 * (h % 2) + 64, 6, 128 * (h // 2):128 * (h // 2) + 128],
                                             ident[0:64, k:k + 1].to_broadcast([64, 64]), rt[0:64, chunk(j)], start=True, stop=True)
                                ins.then_inc(off_done, 1)
                            if i + 1 < len(ITEMS):
                                decay_sums(i + 1, w)
                        for w in state_dirs(j, second):
                            chunk_state(c, j, g, w)
                        pe.wait_ge(xdt_done, 2 * i + 2)
                        pe.wait_ge(m_done, 2 * i + 2)
                        if i:
                            pe.wait_ge(y_done, i)
                        for h in range(GH):
                            for w in range(2):
                                ins = mm(P[64 * (h % 2):64 * (h % 2) + 64, 4, 128 * (h // 2):128 * (h // 2) + 128],
                                         xdt[:, w, 64 * h:64 * h + 64], em[:, w, 128 * h:128 * h + 128], start=(w == 0), stop=(w == 1))
                        ins.then_inc(diag_done, 1)
                pe.wait_ge(y_done, len(ITEMS))
                for f in range(ZT):
                    pe.wait_ge(g_sq, f + 1)
                    for b in range(2):
                        ins = mm(acc(sub["ga"])[:, b, :], ones[:, :], sg[:, f % 2, b * C:(b + 1) * C], start=(f == 0), stop=(f == ZT - 1))
                    ins.then_inc(g_used, 1)

            nh = 0
            for si, sub in enumerate(subplan):
                norm_sum(2 * si, sub["pre_a"])
                pe.wait_ge(xn_ready, 8 * si + 8)
                for p in sub["phases"]:
                    if p.name in ("guA", "guB"):
                        steps(pe, p.N, 0, lambda n, r: unit(p, n, r, xh, xl))
                        nh += p.N // 2
                    elif p.name in ("ain", "aout", "sx", "sz", "sdt", "soutA", "soutB"):
                        if p.name in ("soutA", "soutB"):
                            pe.wait_ge(y_split, KD * (1 + (p.name == "soutB")))
                        rh, rl = (yh, yl) if p.name == "soutB" else (xh, xl)
                        steps(pe, p.N, 0, lambda n, r: unit(p, n, r, rh, rl))
                        if p.name == "sdt":
                            ssd(p, sub)
                        if p.name == "ain":
                            attention(p, sub)
                    else:
                        pe.wait_ge(h_ready, nh + 1)
                        steps(pe, p.N, 0, lambda n, r: unit(p, n, r, hh, hl))
                norm_sum(2 * si + 1, sub["post_a"])


def constants():
    i = np.arange(128)
    rot = np.zeros((128, 128), np.float32)
    for o in range(0, 128, 32):
        for q in range(16):
            rot[o + 16 + q, o + q] = -1.0
            rot[o + q, o + 16 + q] = 1.0
    col = np.arange(64)
    c0 = np.clip(col - 8, 0, 48)
    inside = (col[None] >= c0[:, None]) & (col[None] < c0[:, None] + 16)
    mask = np.tile(np.where(inside, 0.0, NEG), (2, 1))
    return np.concatenate([np.eye(128), (i[:, None] // 64 == i[None] // 64), rot, mask], 1).astype(np.float32)


def rotary_tables():
    t = np.arange(LAT, dtype=np.int32)
    inv = (1.0 / (np.float32(10000.0) ** (np.arange(16, dtype=np.float32) / np.float32(16)))).astype(np.float32)
    f = np.arange(128)
    pos = np.where((f[:, None] % 64) < 32, t[None] // 64, t[None] % 64).astype(np.float32)
    ang = (pos * inv[f % 16][:, None]).astype(np.float32)
    return np.stack([np.cos(ang), np.sin(ang)], 1).astype(np.float32)


def kernel(**inp):
    import concourse.bacc as bacc
    from concourse.bass_utils import run_bass_kernel_spmd as run
    subs = SUBS
    nc = bacc.Bacc("TRN2", target_bir_lowering=False, num_devices=1)
    arrays, d = {}, {}

    def put(name, a):
        a = np.ascontiguousarray(a)
        arrays[name + "_d"] = a
        d[name] = nc.dram_tensor(name + "_d", a.shape, F32, kind="ExternalInput").ap()

    I = {k: np.asarray(v) for k, v in inp.items()}

    def feat(a):
        return a.T.reshape(-1, 128, a.shape[0]).transpose(1, 0, 2)

    def units(w):
        K, N = w.shape
        return w.reshape(K // 128, 128, N // 128, 128).transpose(2, 1, 0, 3).reshape(N // 128, 128, K)

    put("x", feat(np.concatenate([I["x_prompt"][0], I["x_sample"][0]])))
    put("cond", feat(np.stack([I["c_ctx"], I["c"][0]])))
    two = lambda a: np.repeat(a[..., None], 2, axis=-1)
    put("bmod", two(I["b_mod"].reshape(2 * MT, 128).T))
    put("npre", two(I["norm_pre"].reshape(6, KD, 128).transpose(2, 0, 1)))
    put("npost", two(I["norm_post"].reshape(6, KD, 128).transpose(2, 0, 1)))
    put("wmod", np.concatenate([units(w) for w in I["w_mod"]]))
    gu = [np.stack([units(I["ffn_w_gate"][l, f]), units(I["ffn_w_up"][l, f])], 1).reshape(2 * FFT, 128, D)
          for l in range(2) for f in range(2)]
    put("wgu", np.concatenate(gu))
    KA = HALF[0] * 128
    put("wdA", np.concatenate([units(I["ffn_w_down"][l, f][:KA]) for l in range(2) for f in range(2)]))
    put("wdB", np.concatenate([units(I["ffn_w_down"][l, f][KA:]) for l in range(2) for f in range(2)]))
    a_in, a_out = I["attn_w_in"][0], I["attn_w_out"][0]
    pair = lambda a: a.reshape(2, 4, HD, -1).transpose(1, 0, 2, 3).reshape(8 * HD, -1)
    put("ain", units(np.concatenate([pair(a_in[:, :512].T).T, a_in[:, 512:]], 1)))
    put("aout", units(np.concatenate([pair(a_out[:512]), a_out[512:]])))
    put("gqk", np.stack([np.tile(I["attn_q_norm"][0], 2), np.tile(I["attn_k_norm"][0], 2)], 1))
    put("kc", np.concatenate([I["cache_attn_k"].reshape(128, 128), I["cache_na_k"].reshape(128, 512)], 1).T.reshape(5, 128, 128).transpose(1, 0, 2))
    put("vc", np.concatenate([I["cache_attn_v"].reshape(128, 128), I["cache_na_v"].reshape(128, 512)], 1))
    put("cst", constants())
    put("trig", rotary_tables())
    rpb = np.pad(I["na_rpb"][0], ((0, 0), (0, 0), (48, 48)))
    rows = np.stack([rpb[:, :, 63 - c:127 - c] for c in range(64)], 1)
    put("bias", np.concatenate([rows[:, :, 1:15], rows[:, :, 0:14]], 1).reshape(HEADS, 128, 14 * 64))
    s_in, s_out, di = I["ssd_w_in"][0], I["ssd_w_out"][0], 128 * ZT
    cdim = 128 * (XT + BCT)
    put("sz", units(s_in[:, :di]))
    put("sx", units(s_in[:, di:di + cdim]))
    put("sdt", units(np.pad(s_in[:, di + cdim:], ((0, 0), (0, 64)))))
    put("soutA", units(s_out[:D]))
    put("soutB", units(s_out[D:]))
    conv = np.concatenate([I["ssd_conv_w"][0], I["ssd_conv_b"]])
    put("cw", conv.reshape(6, XT + BCT, 128).transpose(2, 1, 0))
    per_tile = lambda a: a.reshape(XT, 128).T
    put("svec", np.concatenate([per_tile(np.repeat(I["ssd_d"][0], HD)), per_tile(I["ssd_norm"][0]),
                                np.tile(I["ssd_a_log"][0].reshape(1, 64), (128, 1)),
                                np.pad(I["ssd_dt_bias"][0], (0, 64))[:, None]], 1))
    put("s0", np.stack([I[n].reshape(2048, 128).T for n in ("state_ssd_fwd", "state_ssd_bwd")]))
    i = np.arange(128)
    a, b = i[:, None], i[None]
    put("tri", np.stack([a <= b, a >= b, a > b, a < b], 1).astype(np.float32))
    d["spill"] = nc.dram_tensor("spill_d", (128, 2048), F32).ap()
    d["zspill"] = nc.dram_tensor("zspill_d", (ZT, 128, T), F32).ap()
    d["s_ctx"] = nc.dram_tensor("s_ctx_d", (2, 128, 2048), F32, kind="ExternalOutput").ap()
    d["kv"] = nc.dram_tensor("kv_d", (128, 10, CTX), F32, kind="ExternalOutput").ap()
    d["y"] = nc.dram_tensor("y_d", (128, KD, T), F32, kind="ExternalOutput").ap()
    build(nc, d, subs)
    r = run(nc, [arrays], core_ids=[0]).results[0]
    y = r["y_d"].transpose(1, 0, 2).reshape(D, T).T
    kv = r["kv_d"].transpose(1, 0, 2).reshape(10 * 128, CTX).T
    cut = lambda a, h: a.reshape(1, 1, CTX, h, HD)
    out = (y[None, :CTX], y[None, CTX:], cut(kv[:, 0:128], 2), cut(kv[:, 128:256], 2), cut(kv[:, 256:768], 8),
           cut(kv[:, 768:1280], 8))
    return out + tuple(r["s_ctx_d"][w].T.reshape(1, 1, 32, HD, 128) for w in range(2))


SUBS = (0, 1, 2, 3, 4, 5)
```

```python
import concourse.bass as bass
from concourse import mybir
from contextlib import ExitStack
import numpy as np

F32 = mybir.dt.float32
F32R = mybir.dt.float32r
ACT = mybir.ActivationFunctionType
ALU = mybir.AluOpType
AXX = mybir.AxisListType.X

D = 1024
KD = D // 128
CTX, LAT = 128, 512
T = CTX + LAT
C = T // 2
FF = 2816
FFT = FF // 128
HALF = (11, 11)
KMAX = max(HALF)
EPS = 1e-6
NMOD = 9
MT = NMOD * KD
HEADS = 8
HD = 64
BLK = T // 128
SLOTS = 4
ZT, XT, BCT = 16, 16, 8


MODS = {0: (22, 8, 22, 0), 2: (22, 8, 22, 0), 3: (22, 2, 0, 0)}
FIRST_MODS = 16
AREA = 93696
NEG = -1e30


class Phase:

    def __init__(self, name, N, nk, q=0):
        self.name, self.N, self.nk, self.q = name, N, nk, q


class Norm:

    def __init__(self, v, a, n, before):
        self.v, self.a, self.n = v, a, n
        self.sq0 = sum(x.n for x in before)
        self.add0 = self.sq0 - len(before)


def plan(subs):
    out, u, a, t, norms = [], 0, 0, FIRST_MODS, []
    for s in subs:
        kind = s % 3
        if kind != 1:
            q1, q2, q3, q4 = MODS.get(s, (0, 0, 0, 0))
            ph = [Phase("guA", 2 * HALF[0], KD, q1), Phase("dnA", KD, HALF[0], q2),
                  Phase("guB", 2 * HALF[1], KD, q3), Phase("dnB", KD, HALF[1], q4)]
        elif s == 1:
            ph = [Phase("ain", 18, KD), Phase("aout", KD, KD)]
        else:
            ph = [Phase("sx", XT + BCT, KD), Phase("sz", ZT, KD), Phase("sdt", 1, KD),
                  Phase("soutA", KD, KD), Phase("soutB", KD, KD)]
        sub = {"s": s, "pre": Norm(len(norms), a, KD, norms), "phases": ph}
        norms.append(sub["pre"])
        a += 1
        for p in ph:
            p.u0, p.a0, p.t0 = u, a, t
            f = 2 * (s // 3) + (s % 3) // 2
            p.w, p.w0 = {"guA": ("wgu", 2 * FFT * f), "guB": ("wgu", 2 * FFT * f + 2 * HALF[0]),
                         "dnA": ("wdA", KD * f), "dnB": ("wdB", KD * f)}.get(p.name, (p.name, 0))
            u, a, t = u + p.N, a + p.N, t + p.q
            if p.name == "ain":
                sub["va"], sub["qa"], sub["ra"] = a, a + 5, a + 10
                a += 15
            if p.name == "sdt":
                sub["gated"] = Norm(len(norms), a, ZT, norms)
                norms.append(sub["gated"])
                a += 1
        sub["post"] = Norm(len(norms), a, KD, norms)
        norms.append(sub["post"])
        a += 1
        out.append(sub)
    phases = [p for sub in out for p in sub["phases"]]
    for p, n in zip(phases, phases[1:] + [None]):
        p.next = n
    return out, t


def steps(eng, N, keep, body):
    rounds = (N - keep) // 4
    if rounds > 1:
        with eng.Fori(0, rounds) as r:
            for j in range(4):
                body(j, r)
    else:
        rounds = 0
    for n in range(4 * rounds, N):
        body(n, 0)


class Steps:

    def __init__(self, eng, sem):
        self.eng, self.sem, self.n, self.i = eng, sem, 0, 0

    def __call__(self, ins):
        ins.then_inc(self.sem, 1)
        self.n += 1

    def wait(self):
        self.eng.wait_ge(self.sem, self.n)


CHUNKS = [(4, False), (3, False), (2, False), (0, True), (1, True), (2, True), (3, True), (4, True)]
GROUPS, GH = 4, 8
ITEMS = [(c, j, g) for c, (j, second) in enumerate(CHUNKS) if second for g in range(GROUPS)]


def state_dirs(j, second):
    if j == 0:
        return (0, 1)
    return ((0,) if j < BLK - 1 else ()) if second else (1,)


STATES = [(c, j, g, w) for c, (j, second) in enumerate(CHUNKS) for g in range(GROUPS) for w in state_dirs(j, second)]


def attention_units():
    def heads(blocks):
        for t in range(4):
            for h in range(2):
                for b in blocks:
                    yield (t, h, b, 4, 64 * h, 0, t, None)
        for t in range(4):
            for h in range(2):
                for b in blocks:
                    yield (6 + t, h, b, 10 + t, 128 * (1 + t) + 64 * h, 1 + t, 4 + t, 2 * t + h if b else None)
    return [*heads([0]), *heads(range(1, BLK))]


def build(nc, d, subs):
    subplan, n_mod = plan(subs)
    phases = [p for sub in subplan for p in sub["phases"]]
    ctx = ExitStack()
    with ctx:
        def sb(name, shape, dt=F32):
            return ctx.enter_context(nc.sbuf_tensor(name, shape, dt))

        def sem(name):
            return ctx.enter_context(nc.semaphore(name))

        x = sb("x", [128, KD, T])
        M0 = (nc.sbuf_base + 31) // 32 * 32
        xh = sb("xh", [128, KD, T], F32R)
        xl = sb("xl", [128, KD, T], F32R)
        raw = sb("raw", [128, 2, KMAX * 128])
        wh = sb("wh", [128, 2, KMAX * 128], F32R)
        wl = sb("wl", [128, 2, KMAX * 128], F32R)
        rts = sb("rts", [128, 2 * T])
        rt, rs = rts[:, 0:T], rts[:, T:2 * T]
        mod = sb("mod", [128, 2 * MT, 2])
        bmod = sb("bmod", [128, 2 * MT, 2])
        npre = sb("npre", [128, 6, KD, 2])
        npost = sb("npost", [128, 6, KD, 2])
        ga = sb("ga", [128, KD, 2])
        gp = sb("gp", [128, KD, 2])
        ones = sb("ones", [128, 128])
        eps = sb("eps", [128, 1])
        tick = sb("tick", [128, 3])
        r5 = sb("r5", [128, 2, BLK])
        mraw = sb("mraw", [128, 2, D])
        A0 = (nc.sbuf_base + 31) // 32 * 32
        area = sb("area", [128, (AREA + 32) // 4])

        def at(name, shape, off, dt=F32):
            return nc.alloc_sbuf_tensor_at(name, shape, dt, offset=A0 + off)

        HB = KMAX * T * 4
        hh = at("hh", [128, KMAX, T], 0, F32R)
        hl = at("hl", [128, KMAX, T], HB, F32R)
        ft = at("ft", [128, KD, T], 61440)
        sg = at("sg", [128, 2, T], 81920)
        ht = at("ht", [128, T], 87040)
        ssq = ht
        sc = (at("sc0", [128, D], 2 * HB), at("sc1", [128, D], 89600))
        cst = sb("cst", [128, 3 * 128 + 64])
        gqk = sb("gqk", [128, 2])
        ident, hones, rotm, wmask = cst[:, 0:128], cst[:, 128:256], cst[:, 256:384], cst[:, 384:448]
        pt = at("pt", [128, 18, T], 0)
        kc = at("kc", [128, 5, 128], 46080)
        vc = at("vc", [128, 5 * 128], 48640)
        trig = at("trig", [128, 2, LAT], 51200)
        vt = at("vt", [128, BLK, 5 * 128], 55296)
        tb = at("tb", [128, 2, 14 * 64], 68096)
        pb = at("pb", [128, 3, T], 75264)
        ptr = at("ptr", [128, 2, T], 82944)
        sbias = at("sbias", [128, 2, T], 88064)
        def at_m(name, shape, off, dt=F32):
            return nc.alloc_sbuf_tensor_at(name, shape, dt, offset=M0 + off)

        xs = at("xs", [128, XT + BCT, T], 0)
        pad = at("pad", [128, 2, T + 8], 61440)
        cv = at("cv", [128, 2, T + 4], 66624)
        zb = at("zb", [128, 2, T], 66624)
        xdt = at("xdt", [128, 2, 512], 61440)
        xw = at("xw", [128, 512], 65536)
        eb = at("eb", [128, 2, 512], 67584)
        cbt = at("cbt", [128, 2, 512], 71680)
        btok = at("btok", [128, 512], 75776)
        so = at("so", [128, 2, 512], 77824)
        tri = at("tri", [128, 4, 128], 81920)
        dtt = at("dtt", [128, BLK, 64], 83968)
        da = at("da", [128, BLK, 64], 85248)
        wdt = at("wdt", [128, 2, BLK, 32], 86528)
        cd = at("cd", [128, BLK, 64], 87808)
        dtr = at("dtr", [128, T], 89088)
        cw = at("cw", [128, 24, 6], 91648)
        svec = at("svec", [128, 2 * XT + 64 + 1], 92224)
        dvec, gvec, arow, dtb = svec[:, 0:XT], svec[:, XT:2 * XT], svec[:, 32:96], svec[:, 96:97]
        zin = at("zin", [128, 2, T], 61440)
        yh = at("yh", [128, KD, T], 40960, F32R)
        yl = at("yl", [128, KD, T], 0, F32R)
        sf = at_m("sf", [128, 2048], 0)
        sbw = at_m("sbw", [128, 2, 2048], 8192)
        rb = at_m("rb", [128, 2, 1024], 24576)
        em = at_m("em", [128, 2, 1024], 32768)
        xtok = mraw[:, :, :].rearrange("p a b -> p (a b)")
        st = sb("st", [128, 4, 4])
        P = ctx.enter_context(nc.psum_tensor("P", [128, 8, 512], F32))

        arrived = [sem("arrived0"), sem("arrived1")]
        m0arrived = [sem("m0arrived0"), sem("m0arrived1")]
        marrived = [sem("marrived0"), sem("marrived1")]
        in_sem = sem("in_sem")
        hi_done = sem("hi_done")
        lo_done = sem("lo_done")
        unit_done = sem("unit_done")
        acc_free = sem("acc_free")
        mod_mac = sem("mod_mac")
        consts = sem("consts")
        sc_in = sem("sc_in")
        silu_c = sem("silu_c")
        own = sem("own")
        sg_done = sem("sg_done")
        hh_done = sem("hh_done")
        h_ready = sem("h_ready")
        sq_done = sem("sq_done")
        ssq_add = sem("ssq_add")
        tot_done = sem("tot_done")
        rt_done = sem("rt_done")
        dg_done = sem("dg_done")
        rb_ready = sem("rb_ready")
        x_ready = sem("x_ready")
        t_done = sem("t_done")
        xh_done = sem("xh_done")
        xn_ready = sem("xn_ready")
        attn_in = sem("attn_in")
        tb_in = [sem("tb_in0"), sem("tb_in1")]
        kv_out = sem("kv_out")
        hq_sq = sem("hq_sq")
        hq_sum = sem("hq_sum")
        hq_root = sem("hq_root")
        hq_norm = sem("hq_norm")
        rot_done = sem("rot_done")
        roped = sem("roped")
        vtr_done = sem("vtr_done")
        qk_done = sem("qk_done")
        nm_done = sem("nm_done")
        p_done = sem("p_done")
        pn_done = sem("pn_done")
        tr_done = sem("tr_done")
        ptr_done = sem("ptr_done")
        pv_done = sem("pv_done")
        o_hi = sem("o_hi")
        o_done = sem("o_done")
        ssd_in = sem("ssd_in")
        st_in = sem("st_in")
        sb_spill = sem("sb_spill")
        sb_back = [sem("sb_back3"), sem("sb_back4")]
        st_out = [sem("st_out0"), sem("st_out1")]
        z_out = [sem("z_out0"), sem("z_out1")]
        z_back = [sem("z_back0"), sem("z_back1")]
        pad_done = sem("pad_done")
        conv_step = sem("conv_step")
        conv_done = sem("conv_done")
        xs_done = sem("xs_done")
        z_done = sem("z_done")
        sp_dve = sem("sp_dve")
        sp_act = sem("sp_act")
        dt_tr = sem("dt_tr")
        da_done = sem("da_done")
        dec_sum = sem("dec_sum")
        dec_exp = sem("dec_exp")
        wdt_done = sem("wdt_done")
        prep_tr = sem("prep_tr")
        prep_cp = sem("prep_cp")
        cb_done = sem("cb_done")
        cbt_done = sem("cbt_done")
        rb_done = sem("rb_done")
        xdt_done = sem("xdt_done")
        xw_done = sem("xw_done")
        seg_done = sem("seg_done")
        e_done = sem("e_done")
        m_done = sem("m_done")
        off_done = sem("off_done")
        eb_done = sem("eb_done")
        offm_done = sem("offm_done")
        diag_done = sem("diag_done")
        s_sum = sem("s_sum")
        s_done = sem("s_done")
        y_done = sem("y_done")
        gated = sem("gated")
        y_split = sem("y_split")
        out_sem = sem("out_sem")
        block = ctx.enter_context(nc.Block())

        def acc(a):
            s = 2 * (a % SLOTS)
            return P[:, s:s + 2, 0:C]

        def two(ap):
            return ap.rearrange("p (b c) -> p b c", b=2)

        def bc_last(ap, n):
            return ap.rearrange("p (a o) -> p a o", o=1).to_broadcast([ap.shape[0], ap.shape[1], n])

        def bc_mid(ap, n):
            return ap.rearrange("p (o b) -> p o b", o=1).to_broadcast([ap.shape[0], n, ap.shape[1]])

        def chunk(j):
            return slice(128 * j, 128 * j + 128)

        def totals(N):
            return flat(N.a % SLOTS)[:, 768:768 + BLK]

        def scale_of(N):
            return flat(N.a % SLOTS)[:, 0:T]

        def flat(s):
            return P[:, 2 * s:2 * s + 2, :].rearrange("p b c -> p (b c)")

        def scores(g):
            return flat(g % 2)

        def one(buf, m, r):
            return buf[:, bass.ds(2 * r + m, 1), :].rearrange("p o t -> p (o t)")

        SIDES = ((0, 0, CTX), (1, CTX, T))

        @block.sync
        def _(sp):
            def load_conditions():
                for c in range(2):
                    sp.dma_start(sc[c][:, :], d["cond"][c]).then_inc(sc_in, 16)

            load_conditions()
            for dst, src in ((bmod[:, :, :], d["bmod"]),
                             (npre[:, :, :, :], d["npre"]), (npost[:, :, :, :], d["npost"]),
                             (cst[:, :], d["cst"]), (x[:, :, :], d["x"])):
                sp.dma_start(dst, src).then_inc(in_sem, 16)

            for t in range(FIRST_MODS):
                if t >= 2:
                    sp.wait_ge(mod_mac, 2 * (t - 1))
                sp.dma_start(mraw[:, t % 2, :], d["wmod"][t]).then_inc(m0arrived[t % 2], 16)

            def unit_source(p, n, r):
                return d[p.w][bass.ds(4 * r + (p.w0 + n), 1), :, :].rearrange("o p n -> (o p) n")

            def load_unit(p, n, r):
                u = p.u0 + n
                if not (isinstance(r, int) and u < 2):
                    sp.wait_ge(lo_done, 4 * r + (u - 1))
                sp.dma_start(raw[:, u % 2, 0:p.nk * 128], unit_source(p, n, r)).then_inc(arrived[u % 2], 16)

            def attention_inputs(before):
                if before:
                    sp.wait_ge(unit_done, before)
                for dst, src in ((gqk[:, :], d["gqk"]), (kc[:, :, :], d["kc"]),
                                 (vc[:, :], d["vc"]), (trig[:, :, :], d["trig"])):
                    sp.dma_start(dst, src).then_inc(attn_in, 16)

            def ssd_inputs(idx):
                sp.wait_ge(xn_ready, 8 * (idx + 1))
                for dst, src in ((tri[:, :, :], d["tri"]), (cw[:, :, :], d["cw"]), (svec[:, :], d["svec"])):
                    sp.dma_start(dst, src).then_inc(ssd_in, 16)

            def ssd_states(p):
                sp.wait_ge(unit_done, p.u0)
                sp.dma_start(sf[:, :], d["s0"][0]).then_inc(st_in, 16)
                sp.dma_start(sbw[:, 0, :], d["s0"][1]).then_inc(st_in, 16)
                sp.wait_ge(s_done, GROUPS)
                sp.dma_start(d["spill"], sbw[:, 1, :]).then_inc(sb_spill, 16)
                n_ctx = sum(1 for c, *_ in STATES if c < 3)
                for i, (_, _, g, w) in enumerate([x for x in STATES if x[1] == 0]):
                    sp.wait_ge(s_done, n_ctx + i + 1)
                    sp.dma_start(d["s_ctx"][w][:, 512 * g:512 * g + 512], so[:, i % 2, :]).then_inc(st_out[i % 2], 16)
                sp.wait_ge(sb_spill, 16)
                sp.wait_ge(off_done, 2 * GROUPS)
                sp.dma_start(sbw[:, 1, :], d["spill"]).then_inc(sb_back[0], 16)
                sp.wait_ge(off_done, 4 * GROUPS)
                sp.dma_start(sbw[:, 0, :], d["s0"][1]).then_inc(sb_back[1], 16)
                sp.wait_ge(y_done, len(ITEMS))
                for f in range(ZT):
                    if f >= 2:
                        sp.wait_ge(gated, f - 1)
                    sp.wait_ge(z_out[f % 2], 16 * (ZT // 2))
                    sp.dma_start(zin[:, f % 2, :], d["zspill"][f]).then_inc(z_back[f % 2], 16)

            second = next((sub["phases"][0] for sub in subplan if sub["s"] == 2), None)
            for p in phases:
                if p is second:
                    sp.wait_ge(unit_done, p.u0 - KD + 1)
                    load_conditions()
                if p.name == "soutA":
                    load_unit(p, 0, 0)
                    load_unit(p, 1, 0)
                    ssd_states(p)
                    for n in range(2, p.N):
                        load_unit(p, n, 0)
                elif p.u0 == 0 or p.name in ("ain", "sx"):
                    for n in range(4):
                        load_unit(p, n, 0)
                        if n == 1 and p.name == "ain":
                            attention_inputs(p.u0)
                        if n == 1 and p.name == "sx":
                            ssd_inputs([sub["s"] for sub in subplan].index(4))
                    rounds = p.N // 4
                    with sp.Fori(1, rounds) as r:
                        for j in range(4):
                            load_unit(p, j, r)
                    for n in range(4 * rounds, p.N):
                        load_unit(p, n, 0)
                else:
                    steps(sp, p.N, 0, lambda n, r: load_unit(p, n, r))
            sp.wait_ge(x_ready, 8 * len(subplan))
            sp.dma_start(d["y"], x[:, :, :]).then_inc(out_sem, 16)
            sp.wait_ge(out_sem, 16)

        @block.gpsimd
        def _(pool):
            G = nc.gpsimd

            def add_squares(N):
                for k in range(1, N.n):
                    pool.wait_ge(sq_done, N.sq0 + k + 1)
                    if k > 1:
                        pool.wait_ge(ssq_add, N.add0 + k - 1)
                    G.tensor_tensor(ssq[:, :], ssq[:, :], sg[:, k % 2, :], ALU.add).then_inc(ssq_add, 1)

            def load_mods(t0, t1):
                if t1 > t0:
                    with pool.Fori(t0 // 2, t1 // 2) as r:
                        for t in range(2):
                            pool.wait_ge(mod_mac, 4 * r + 2 * (t - 1))
                            load_mod(t, r)

            def load_mod(t, r):
                pool.dma_start(mraw[:, t, :], d["wmod"][bass.ds(2 * r + t, 1), :, :].rearrange("o p n -> (o p) n")
                               ).then_inc(marrived[t], 16)

            def ssd():
                pool.wait_ge(ssd_in, 48)
                pool.wait_ge(da_done, 1)
                pool.wait_ge(wdt_done, 1)
                for b in range(2):
                    pool.wait_ge(z_out[b], 16 * (ZT // 2))

                def decay_operand(i):
                    c, j, g = ITEMS[i]
                    for w in range(2):
                        if i:
                            pool.wait_ge(seg_done, 2 * (i - 1) + w + 1)
                        G.tensor_tensor(rb[:, w, :].rearrange("p (h l) -> p h l", h=GH), bc_mid(tri[:, w, :], GH),
                                        bc_last(da[:, j, 32 * w + GH * g:32 * w + GH * g + GH], 128), ALU.mult).then_inc(rb_done, 1)

                def weighted(c, j, g, w):
                    n = STATES.index((c, j, g, w))
                    if n:
                        pool.wait_ge(s_sum, n)
                    G.tensor_tensor(xw[:, :].rearrange("p (h q) -> p h q", h=GH),
                                    xtok[:, 512 * g:512 * g + 512].rearrange("p (h q) -> p h q", h=GH),
                                    bc_last(wdt[:, w, j, GH * g:GH * g + GH], HD), ALU.mult).then_inc(xw_done, 1)

                for c, (j, second) in enumerate(CHUNKS):
                    if c == 2:
                        decay_operand(0)
                    pool.wait_ge(prep_cp, 5 * (c + 1))
                    for g in range(GROUPS):
                        if second:
                            i = ITEMS.index((c, j, g))
                            if i + 1 < len(ITEMS):
                                decay_operand(i + 1)
                            for w in range(2):
                                if i:
                                    pool.wait_ge(diag_done, i)
                                G.tensor_tensor(xdt[:, w, :].rearrange("p (h q) -> p h q", h=GH),
                                                xtok[:, 512 * g:512 * g + 512].rearrange("p (h q) -> p h q", h=GH),
                                                bc_last(dtt[:, j, 32 * w + GH * g:32 * w + GH * g + GH], HD),
                                                ALU.mult).then_inc(xdt_done, 1)
                        for w in state_dirs(j, second):
                            weighted(c, j, g, w)

            for sub in subplan:
                add_squares(sub["pre"])
                for p in sub["phases"]:
                    load_mods(p.t0, p.t0 + p.q)
                    if p.name == "sdt":
                        ssd()
                        add_squares(sub["gated"])
                add_squares(sub["post"])

        @block.scalar
        def _(act):
            act.wait_ge(in_sem, 16 * 5)

            def high(p, n, r):
                u = p.u0 + n
                act.wait_ge(arrived[u % 2], r * 32 + 16 * (u // 2 + 1))
                nc.scalar.copy(wh[:, u % 2, 0:p.nk * 128], raw[:, u % 2, 0:p.nk * 128]).then_inc(hi_done, 1)

            def ahead(p, n, r):
                if n + 2 < p.N or not isinstance(r, int):
                    high(p, n + 2, r)
                elif p.next is not None:
                    k = n + 2 - p.N
                    high(*((p.next, k) if k < p.next.N else (p.next.next, k - p.next.N)), 0)

            def square(N, src, k):
                if k == 0:
                    dst = ssq[:, :]
                else:
                    dst = sg[:, k % 2, :]
                    if k >= 3:
                        act.wait_ge(ssq_add, N.add0 + k - 2)
                nc.scalar.square(dst, src[:, k, :]).then_inc(sq_done, 1)

            def root(N):
                act.wait_ge(tot_done, N.v + 1)
                act.wait_ge(consts, 1)
                nc.scalar.activation(r5[:, 0, :], totals(N), ACT.Sqrt, bias=eps[:, 0:1], scale=1.0 / (128 * N.n)).then_inc(rt_done, 1)

            units = attention_units()

            def load_bias(h):
                act.dma_start(tb[:, h % 2, :], d["bias"][h]).then_inc(tb_in[h % 2], 16)

            def attention(p, sub):
                act.wait_ge(attn_in, 16 * 4)
                for k in range(5):
                    act.wait_ge(acc_free, SLOTS + p.a0 + k + 1)
                    if k >= 2:
                        act.wait_ge(hq_sum, k - 1)
                    nc.scalar.square(pb[:, k % 2, :], pt[:, k, :]).then_inc(hq_sq, 1)
                    if k >= 1:
                        head_root(k - 1, sub)
                head_root(4, sub)
                act.wait_ge(hq_norm, 5)
                act.wait_ge(acc_free, SLOTS + p.a0 + p.N)
                act.dma_start(d["kv"][:, 0:2, :], pt[:, 4:6, 0:CTX]).then_inc(kv_out, 16)
                act.dma_start(d["kv"][:, 2:10, :], pt[:, 10:18, 0:CTX]).then_inc(kv_out, 16)
                load_bias(0)
                load_bias(1)
                for g in range(len(units) + 2):
                    if g < len(units):
                        b, bias = units[g][2], units[g][7]
                        n = T if b else CTX
                        act.wait_ge(nm_done, g + 1)
                        if g >= 3:
                            act.wait_ge(tr_done, g - 2)
                        if bias is None:
                            act.wait_ge(qk_done, g + 1)
                            src, scale = scores(g)[:, 0:n], HD ** -0.5
                        else:
                            src, scale = sbias[:, g % 2, :], 1.0
                        nc.scalar.activation(pb[:, g % 3, 0:n], src, ACT.Exp, bias=st[:, 1, g % 4:g % 4 + 1],
                                             scale=scale, accum_out=st[:, 2, g % 4:g % 4 + 1]).then_inc(p_done, 1)
                        if bias is not None and b == BLK - 1 and bias + 2 < HEADS:
                            load_bias(bias + 2)
                    if g >= 2:
                        h = g - 2
                        n = T if units[h][2] else CTX
                        act.wait_ge(tr_done, h + 1)
                        if h >= 2:
                            act.wait_ge(pv_done, h - 1)
                        nc.scalar.copy(ptr[:, h % 2, 0:n], flat(2)[:, 0:n]).then_inc(ptr_done, 1)

            def ssd(sub):
                A = nc.scalar.activation
                act.wait_ge(sp_dve, 1)
                A(em[0:64, 0, 0:T], rb[0:64, 0, 0:T], ACT.Exp).then_inc(sp_act, 1)
                act.wait_ge(sp_dve, 2)
                A(rb[0:64, 1, 0:T], em[0:64, 1, 0:T], ACT.Ln).then_inc(sp_act, 1)
                act.wait_ge(ssd_in, 48)
                A(arow, arow, ACT.Exp).then_inc(sp_act, 1)
                act.wait_ge(dec_sum, 1)
                nc.scalar.copy(rt[0:64, :], flat(0)[0:64, 0:T]).then_inc(dec_exp, 1)
                A(wdt[:, :, :, :], P[:, 2, 0:320].rearrange("p (w j h) -> p w j h", w=2, j=BLK), ACT.Exp).then_inc(dec_exp, 1)
                for b in range(2):
                    act.wait_ge(z_out[b], 16 * (ZT // 2))
                A(cd[:, :, :], P[:, 3, 0:320].rearrange("p (j h) -> p j h", j=BLK), ACT.Exp).then_inc(dec_exp, 1)

                def decays(i):
                    for w in range(2):
                        act.wait_ge(seg_done, 2 * i + w + 1)
                        if i:
                            act.wait_ge(diag_done, i)
                        A(em[:, w, :], P[:, 2 * w:2 * w + 2, :].rearrange("p b c -> p (b c)"), ACT.Exp).then_inc(e_done, 1)

                for c, (j, second) in enumerate(CHUNKS):
                    for k in range(5):
                        act.wait_ge(prep_tr, 5 * c + k + 1)
                        if c:
                            if k < 4:
                                act.wait_ge(xw_done, sum(1 for x in STATES if x[0] < c))
                                act.wait_ge(xdt_done, 2 * sum(1 for x in ITEMS if x[0] < c)) if c > 3 else None
                            else:
                                act.wait_ge(s_sum, sum(1 for x in STATES if x[0] < c))
                        dst = xtok[:, 512 * k:512 * k + 512] if k < 4 else btok[:, :]
                        nc.scalar.copy(dst, P[:, 6 + k % 2, :]).then_inc(prep_cp, 1)
                    if not second:
                        continue
                    for g in range(GROUPS):
                        i = ITEMS.index((c, j, g))
                        decays(i)
                        if j:
                            for w in range(2):
                                n = 2 * (i - GROUPS) + w
                                act.wait_ge(off_done, n + 1)
                                if i > GROUPS:
                                    act.wait_ge(y_done, i)
                                A(eb[:, w, :], P[:, 6, :], ACT.Exp).then_inc(eb_done, 1)
                for f in range(ZT):
                    act.wait_ge(gated, f + 1)
                    square(sub["gated"], xs, f)
                root(sub["gated"])

            def head_root(k, sub):
                act.wait_ge(hq_sum, k + 1)
                if k >= 2:
                    act.wait_ge(acc_free, SLOTS + sub["qa"] + k - 1)
                nc.scalar.activation(two(sbias[:, k % 2, :]), acc(sub["qa"] + k), ACT.Sqrt, bias=eps[:, 0:1],
                                     scale=1.0 / HD).then_inc(hq_root, 1)

            for si, sub in enumerate(subplan):
                s = sub["s"]
                if s in (0, 2):
                    act.wait_ge(sc_in, 32 * (1 + (s > 0)))
                    for c in range(2):
                        nc.scalar.activation(sc[c][:, :], sc[c][:, :], ACT.Silu).then_inc(silu_c, 1)
                for k in range(KD):
                    if si:
                        act.wait_ge(x_ready, 8 * (si - 1) + k + 1)
                    square(sub["pre"], x, k)
                root(sub["pre"])
                if si == 0:
                    high(phases[0], 0, 0)
                    high(phases[0], 1, 0)
                lay, j = s // 3, s % 3
                for k in range(KD):
                    act.wait_ge(t_done, 2 * (8 * si + k) + 2)
                    for c, t0, t1 in SIDES:
                        ins = nc.scalar.activation(xh[:, k, t0:t1], ft[:, k, t0:t1], ACT.Identity,
                                                   bias=mod[:, lay * MT + 3 * j * KD + k, c:c + 1])
                    ins.then_inc(xh_done, 1)
                for p in sub["phases"]:
                    if p.name in ("guA", "guB"):
                        def step(n, r):
                            act.wait_ge(unit_done, 4 * r + (p.u0 + n + 1))
                            ahead(p, n, r)
                            if n % 2 == 0:
                                nc.scalar.activation(two(sg[:, (n // 2) % 2, :]), acc(p.a0 + n), ACT.Silu
                                                     ).then_inc(sg_done, 1)
                        steps(act, p.N, 2, step)
                    elif p.name == "sx":
                        def step(n, r):
                            act.wait_ge(unit_done, 4 * r + (p.u0 + n + 1))
                            a, b = p.a0 + n, n % 2
                            act.wait_ge(conv_done, 4 * r + (n + 1))
                            nc.scalar.copy(pad[:, b, 2:2 + CTX], acc(a)[:, 0, 0:CTX])
                            nc.scalar.copy(pad[:, b, CTX + 6:C + 6], acc(a)[:, 0, CTX:C])
                            nc.scalar.copy(pad[:, b, C + 6:T + 6], acc(a)[:, 1, :]).then_inc(pad_done, 1)
                            ahead(p, n, r)
                            act.wait_ge(conv_done, 4 * r + (n + 3))
                            out = one(xs, n, 2 * r)
                            nc.scalar.activation(out[:, 0:CTX], cv[:, b, 0:CTX], ACT.Silu)
                            nc.scalar.activation(out[:, CTX:T], cv[:, b, CTX + 4:T + 4], ACT.Silu).then_inc(xs_done, 1)
                        steps(act, p.N, 2, step)
                        act.wait_ge(xs_done, XT + BCT + 2)
                    elif p.name == "sz":
                        for n in range(p.N):
                            act.wait_ge(unit_done, p.u0 + n + 1)
                            ahead(p, n, 0)
                            if n >= 2:
                                act.wait_ge(z_out[n % 2], 16 * (n // 2))
                            nc.scalar.activation(two(zb[:, n % 2, :]), acc(p.a0 + n), ACT.Silu).then_inc(z_done, 1)
                            act.wait_ge(z_done, n + 1)
                            act.dma_start(d["zspill"][n], zb[:, n % 2, :]).then_inc(z_out[n % 2], 16)
                    elif p.name == "sdt":
                        act.wait_ge(unit_done, p.u0 + 1)
                        high(p.next, 1, 0)
                        ssd(sub)
                    elif p is sub["phases"][-1]:
                        for n in range(p.N):
                            act.wait_ge(unit_done, p.u0 + n + 1)
                            ahead(p, n, 0)
                            if n:
                                act.wait_ge(acc_free, SLOTS + p.a0 + n)
                                square(sub["post"], ft, n - 1)
                    else:
                        def step(n, r):
                            act.wait_ge(unit_done, 4 * r + (p.u0 + n + 1))
                            ahead(p, n, r)
                        steps(act, p.N, 2, step)
                    if p.name == "ain":
                        attention(p, sub)
                act.wait_ge(acc_free, SLOTS + p.a0 + KD)
                square(sub["post"], ft, KD - 1)
                root(sub["post"])

        @block.vector
        def _(dve):
            V = nc.vector
            me = Steps(dve, own)
            V.memset(ones[:, :], 1.0)
            V.memset(eps[:, :], EPS).then_inc(consts, 1)
            dve.wait_ge(consts, 1)
            V.memset(tick[:, 1:2], 0.0).then_inc(acc_free, SLOTS)
            V.memset(tick[:, 0:1], 0.0).then_inc(h_ready, 1)
            dve.wait_ge(in_sem, 16 * 5)

            def low(p, n, r):
                u = p.u0 + n
                dve.wait_ge(arrived[u % 2], r * 32 + 16 * (u // 2 + 1))
                dve.wait_ge(hi_done, 4 * r + (u + 1))
                V.tensor_tensor(wl[:, u % 2, 0:p.nk * 128], raw[:, u % 2, 0:p.nk * 128],
                                wh[:, u % 2, 0:p.nk * 128].bitcast(F32), ALU.subtract).then_inc(lo_done, 1)

            def ahead(p, n, r):
                if n + 2 < p.N or not isinstance(r, int):
                    low(p, n + 2, r)
                elif p.next is not None:
                    k = n + 2 - p.N
                    low(*((p.next, k) if k < p.next.N else (p.next.next, k - p.next.N)), 0)

            def norm_scale(N):
                dve.wait_ge(rt_done, N.v + 1)
                me(V.reciprocal(r5[:, 1, :], r5[:, 0, :]))
                me.wait()
                V.tensor_tensor(rs[:, :].rearrange("p (b c) -> p b c", b=BLK), bc_mid(ident, BLK),
                                bc_last(r5[:, 1, :], 128), ALU.mult).then_inc(dg_done, 1)
                dve.wait_ge(rb_ready, N.v + 1)
                return scale_of(N)

            def free_scale(N):
                V.memset(tick[:, 0:1], 0.0).then_inc(acc_free, 1)
                dve.wait_ge(acc_free, SLOTS + N.a + 1)

            def mod_tile(t, r=0):
                if t < FIRST_MODS:
                    dve.wait_ge(m0arrived[t % 2], 16 * (t // 2 + 1))
                else:
                    dve.wait_ge(marrived[t % 2], 32 * r + 16 * ((t - FIRST_MODS) // 2 + 1))
                if t:
                    dve.wait_ge(mod_mac, 8 * r + 2 * t)
                w = mraw[:, t % 2, :]
                for c in range(2):
                    V.scalar_tensor_tensor(rts[:, 0:D] if c == 0 else w, w, 1.0, sc[c][:, :], ALU.mult, ALU.mult,
                                           accum_out=mod[:, bass.ds(4 * r + t, 1), c:c + 1].rearrange("p o c -> p (o c)")
                                           ).then_inc(mod_mac, 1)

            units = attention_units()

            def attention(p, sub):
                dve.wait_ge(attn_in, 16 * 4)
                for f in range(5):
                    dve.wait_ge(vtr_done, f + 1)
                    V.tensor_copy(vt[:, :, 128 * f:128 * f + 128],
                                  flat((sub["va"] + f) % SLOTS)[:, 0:T].rearrange("p (b c) -> p b c", b=BLK)).then_inc(acc_free, 1)
                dve.wait_ge(acc_free, SLOTS + p.a0 + p.N)
                for k in range(5):
                    dve.wait_ge(hq_root, k + 1)
                    if k:
                        dve.wait_ge(hq_norm, k)
                    V.reciprocal(rs[:, :], sbias[:, k % 2, :]).then_inc(acc_free, 1)
                    dve.wait_ge(acc_free, SLOTS + sub["qa"] + k + 1)
                    V.scalar_tensor_tensor(pt[:, k, :], pt[:, k, :], gqk[:, k // 4:k // 4 + 1], rs[:, :],
                                           ALU.mult, ALU.mult).then_inc(hq_norm, 1)
                for k in range(5):
                    dve.wait_ge(rot_done, k + 1)
                    if k == 0:
                        dve.wait_ge(hq_norm, 5)
                    V.tensor_tensor(ptr[:, 0, 0:LAT], flat((sub["ra"] + k) % SLOTS)[:, 0:LAT], trig[:, 1, :], ALU.mult).then_inc(acc_free, 1)
                    me(V.tensor_tensor(pt[:, k, CTX:T], pt[:, k, CTX:T], trig[:, 0, :], ALU.mult))
                    me.wait()
                    dve.wait_ge(acc_free, SLOTS + sub["ra"] + k + 1)
                    V.tensor_tensor(pt[:, k, CTX:T], pt[:, k, CTX:T], ptr[:, 0, 0:LAT], ALU.add).then_inc(roped, 1)
                    dve.wait_ge(roped, k + 1)
                for g in range(len(units) + 3):
                    if g < len(units):
                        front(g)
                    if 1 <= g <= len(units):
                        h = g - 1
                        n = T if units[h][2] else CTX
                        dve.wait_ge(p_done, h + 1)
                        me(V.reciprocal(st[:, 3, h % 4:h % 4 + 1], st[:, 2, h % 4:h % 4 + 1]))
                        me.wait()
                        V.tensor_scalar(pb[:, h % 3, 0:n], pb[:, h % 3, 0:n], st[:, 3, h % 4:h % 4 + 1], None,
                                        ALU.mult).then_inc(pn_done, 1)
                    if g >= 3:
                        h = g - 3
                        _, half, b, _, _, _, to, _ = units[h]
                        rows, cols = slice(64 * half, 64 * half + 64), slice(128 * b, 128 * b + 128)
                        dve.wait_ge(pv_done, h + 1)
                        V.tensor_copy(xh[rows, to, cols], P[rows, 6 + h % 2, 0:128]).then_inc(o_hi, 1)
                        dve.wait_ge(o_hi, h + 1)
                        V.tensor_tensor(xl[rows, to, cols], P[rows, 6 + h % 2, 0:128], xh[rows, to, cols].bitcast(F32),
                                        ALU.subtract).then_inc(o_done, 1)
                dve.wait_ge(kv_out, 32)

            def ssd(p, sub):
                v, m, e, u = dtr[0:64, :], rs[0:64, :], em[0:64, 0, 0:T], em[0:64, 1, 0:T]
                neg, ln = rb[0:64, 0, 0:T], rb[0:64, 1, 0:T]
                dve.wait_ge(acc_free, SLOTS + p.a0 + 1)
                me(V.tensor_scalar(m, v, 0.0, None, ALU.max))
                me(V.tensor_scalar(neg, v, -1.0, None, ALU.mult))
                me.wait()
                V.tensor_tensor(neg, neg, v, ALU.min).then_inc(sp_dve, 1)
                dve.wait_ge(sp_act, 1)
                V.tensor_scalar(u, e, 1.0, None, ALU.add).then_inc(sp_dve, 1)
                dve.wait_ge(sp_dve, 2)
                me(V.tensor_scalar(neg, u, -1.0, 1e-30, ALU.add, ALU.max))
                me.wait()
                me(V.tensor_scalar(v, neg, 1e-30, None, ALU.is_equal))
                me(V.reciprocal(neg, neg))
                me.wait()
                dve.wait_ge(sp_act, 2)
                me(V.tensor_tensor(neg, neg, ln, ALU.mult))
                me.wait()
                me(V.tensor_tensor(neg, neg, v, ALU.add))
                me.wait()
                me(V.tensor_tensor(neg, neg, e, ALU.mult))
                me.wait()
                me(V.tensor_tensor(v, neg, m, ALU.add))
                me.wait()
                V.memset(tick[:, 0:1], 0.0).then_inc(sp_dve, 1)
                dve.wait_ge(dt_tr, 1)
                me(V.tensor_copy(dtt[:, :, :], P[:, 7, 0:320].rearrange("p (j h) -> p j h", j=BLK)))
                me.wait()
                dve.wait_ge(sp_act, 3)
                V.scalar_tensor_tensor(da[:, :, :], dtt[:, :, :], -1.0, bc_mid(arow, BLK), ALU.mult, ALU.mult).then_inc(da_done, 1)
                dve.wait_ge(dec_exp, 3)
                for w in range(2):
                    ins = V.tensor_tensor(wdt[:, w, :, :], wdt[:, w, :, :], dtt[:, :, 32 * w:32 * w + 32], ALU.mult)
                ins.then_inc(wdt_done, 1)
                dve.wait_ge(st_in, 32)
                for b in range(2):
                    dve.wait_ge(z_out[b], 16 * (ZT // 2))

                def take_state(c, j, g, w):
                    n = STATES.index((c, j, g, w))
                    cols = slice(512 * g, 512 * g + 512)
                    heads = lambda ap: ap.rearrange("p (h q) -> p h q", h=GH)
                    dve.wait_ge(s_sum, n + 1)
                    if j == 0:
                        k = 2 * g + w
                        if k >= 2:
                            dve.wait_ge(st_out[k % 2], 16 * (k // 2))
                        V.tensor_copy(so[:, k % 2, :], P[:, 7, :]).then_inc(s_done, 1)
                        return
                    decay = bc_last(cd[:, j, 32 * w + GH * g:32 * w + GH * g + GH], HD)
                    if w == 0:
                        src = dst = sf[:, cols]
                    else:
                        src, dst = sbw[:, (4 - j) % 2, cols], sbw[:, (5 - j) % 2, cols]
                        if j == 2 and g == 0:
                            dve.wait_ge(sb_spill, 16)
                    me.wait()
                    dve.wait_ge(s_done, n) if n else None
                    me(V.tensor_tensor(heads(dst), heads(src), decay, ALU.mult))
                    me.wait()
                    V.tensor_tensor(dst, dst, P[:, 7, :], ALU.add).then_inc(s_done, 1)

                for c, (j, second) in enumerate(CHUNKS):
                    if not second:
                        for g in range(GROUPS):
                            take_state(c, j, g, 1)
                        continue
                    dve.wait_ge(cb_done, c - 2)
                    if ITEMS[0][0] != c:
                        dve.wait_ge(m_done, 2 * ITEMS.index((c, j, 0)))
                    for w in range(2):
                        V.tensor_tensor(cbt[:, w, :].rearrange("p (g l) -> p g l", g=GROUPS),
                                        P[:, 7, :].rearrange("p (g l) -> p g l", g=GROUPS),
                                        bc_mid(tri[:, w, :], GROUPS), ALU.mult).then_inc(cbt_done, 1)
                    dve.wait_ge(cbt_done, 2 * (c - 2))
                    for g in range(GROUPS):
                        i = ITEMS.index((c, j, g))
                        for w in range(2):
                            dve.wait_ge(e_done, 2 * i + w + 1)
                            m3 = em[:, w, :].rearrange("p (h l) -> p h l", h=GH)
                            V.tensor_tensor(m3, m3, bc_mid(cbt[:, w, 128 * g:128 * g + 128], GH), ALU.mult).then_inc(m_done, 1)
                        if j:
                            for w in range(2):
                                n = 2 * (i - GROUPS) + w
                                dve.wait_ge(eb_done, n + 1)
                                V.tensor_tensor(eb[:, w, :], eb[:, w, :], P[:, 5, :], ALU.mult).then_inc(offm_done, 1)
                        for w in state_dirs(j, second):
                            take_state(c, j, g, w)
                        y = xs[:, 4 * g:4 * g + 4, chunk(j)]
                        q4 = lambda ap: ap.rearrange("p (q l) -> p q l", q=4)
                        me(V.tensor_tensor(y, y, bc_last(dvec[:, 4 * g:4 * g + 4], 128), ALU.mult))
                        me.wait()
                        if j:
                            dve.wait_ge(offm_done, 2 * (i - GROUPS) + 2)
                            for w in range(2):
                                me(V.tensor_tensor(y, y, q4(eb[:, w, :]), ALU.add))
                                me.wait()
                        dve.wait_ge(diag_done, i + 1)
                        V.tensor_tensor(y, y, q4(P[:, 4, :]), ALU.add).then_inc(y_done, 1)
                        dve.wait_ge(y_done, i + 1)
                for f in range(ZT):
                    dve.wait_ge(z_back[f % 2], 16 * (f // 2 + 1))
                    V.tensor_tensor(xs[:, f, :], xs[:, f, :], zin[:, f % 2, :], ALU.mult).then_inc(gated, 1)
                scale = norm_scale(sub["gated"])
                dve.wait_ge(gated, ZT)
                for f in range(ZT):
                    h, l = (xh, xl) if f < KD else (yh, yl)
                    me(V.scalar_tensor_tensor(xs[:, f, :], xs[:, f, :], gvec[:, f:f + 1], scale, ALU.mult, ALU.mult))
                    me.wait()
                    me(V.tensor_copy(h[:, f % KD, :], xs[:, f, :]))
                    me.wait()
                    V.tensor_tensor(l[:, f % KD, :], xs[:, f, :], h[:, f % KD, :].bitcast(F32), ALU.subtract).then_inc(y_split, 1)
                    dve.wait_ge(y_split, f + 1)
                free_scale(sub["gated"])

            def front(g):
                b, bias = units[g][2], units[g][7]
                n = T if b else CTX
                mx, nm = st[:, 0, g % 4:g % 4 + 1], st[:, 1, g % 4:g % 4 + 1]
                if bias is not None and b == 1:
                    dve.wait_ge(tb_in[bias % 2], 16 * (bias // 2 + 1))
                    slot = tb[:, bias % 2, :].rearrange("p (m c) -> p m c", c=64)
                    me(V.tensor_tensor(slot, slot, wmask.rearrange("p (o c) -> p o c", o=1).to_broadcast([128, 14, 64]), ALU.add))
                    me.wait()
                dve.wait_ge(qk_done, g + 1)
                if bias is None:
                    me(V.reduce_max(mx, scores(g)[:, 0:n], AXX))
                    me.wait()
                    V.tensor_scalar(nm, mx, -HD ** -0.5, None, ALU.mult).then_inc(nm_done, 1)
                else:
                    if g >= 2:
                        dve.wait_ge(p_done, g - 1)
                    m0 = 64 * (6 - 2 * (b - 1))
                    me(V.scalar_tensor_tensor(sbias[:, g % 2, 0:LAT], scores(g)[:, 0:LAT], HD ** -0.5,
                                              tb[:, bias % 2, m0:m0 + LAT], ALU.mult, ALU.add))
                    me(V.tensor_scalar(sbias[:, g % 2, LAT:T], scores(g)[:, LAT:T], HD ** -0.5, None, ALU.mult))
                    me.wait()
                    me(V.reduce_max(mx, sbias[:, g % 2, :], AXX))
                    me.wait()
                    V.tensor_scalar(nm, mx, -1.0, None, ALU.mult).then_inc(nm_done, 1)

            dve.wait_ge(silu_c, 2)
            for t in range(FIRST_MODS):
                mod_tile(t)
            for si, sub in enumerate(subplan):
                s = sub["s"]
                lay, j = s // 3, s % 3
                m0 = lay * MT + 3 * j * KD
                dve.wait_ge(mod_mac, 2 * sub["phases"][0].t0)
                me(V.tensor_tensor(mod[:, m0:m0 + 2 * KD, :], mod[:, m0:m0 + 2 * KD, :], bmod[:, m0:m0 + 2 * KD, :], ALU.add))
                me.wait()
                me(V.scalar_tensor_tensor(ga[:, :, :], mod[:, m0 + KD:m0 + 2 * KD, :], 1.0, npre[:, s, :, :], ALU.add, ALU.mult))
                me.wait()
                scale = norm_scale(sub["pre"])
                if si:
                    dve.wait_ge(x_ready, 8 * si)
                else:
                    low(phases[0], 0, 0)
                    low(phases[0], 1, 0)

                def scaled(k):
                    for c, t0, t1 in SIDES:
                        V.scalar_tensor_tensor(ft[:, k, t0:t1], x[:, k, t0:t1], ga[:, k, c:c + 1], scale[:, t0:t1],
                                               ALU.mult, ALU.mult).then_inc(t_done, 1)

                def lows(k):
                    dve.wait_ge(xh_done, 8 * si + k + 1)
                    for c, t0, t1 in SIDES:
                        ins = V.scalar_tensor_tensor(xl[:, k, t0:t1], ft[:, k, t0:t1], mod[:, m0 + k, c:c + 1],
                                                     xh[:, k, t0:t1].bitcast(F32), ALU.add, ALU.subtract)
                    ins.then_inc(xn_ready, 1)

                for k in range(KD):
                    scaled(k)
                    if k >= 1:
                        dve.wait_ge(t_done, 2 * (8 * si + k))
                        lows(k - 1)
                dve.wait_ge(t_done, 2 * (8 * si + KD))
                free_scale(sub["pre"])
                lows(KD - 1)
                dve.wait_ge(silu_c, 2 if s < 2 else 4)
                for p in sub["phases"]:
                    if p.name in ("guA", "guB"):
                        hm0 = sum(HALF) * sum(1 for q in subplan[:si] if q["s"] % 3 != 1) + (HALF[0] if p.name == "guB" else 0)

                        def step(n, r):
                            dve.wait_ge(unit_done, 4 * r + (p.u0 + n + 1))
                            ahead(p, n, r)
                            if n % 2:
                                m, a = n // 2, p.a0 + n
                                dve.wait_ge(sg_done, 2 * r + (hm0 + m + 1))
                                dve.wait_ge(h_ready, 2 * r + (hm0 + m + 1))
                                V.tensor_tensor(two(ht[:, :]), acc(a), two(sg[:, m % 2, :]), ALU.mult).then_inc(acc_free, 2)
                                dve.wait_ge(acc_free, 4 * r + (SLOTS + a + 1))
                                V.tensor_copy(one(hh, m, r), ht[:, :]).then_inc(hh_done, 1)
                                dve.wait_ge(hh_done, 2 * r + (hm0 + m + 1))
                                V.tensor_tensor(one(hl, m, r), ht[:, :], one(hh, m, r).bitcast(F32),
                                                ALU.subtract).then_inc(h_ready, 1)
                            if n < p.q:
                                mod_tile(p.t0 + n, r)
                        steps(dve, p.N, 2, step)
                    elif p.name == "sx":
                        dve.wait_ge(ssd_in, 48)
                        me(V.memset(pad[:, :, :], 0.0))
                        me.wait()
                        V.memset(tick[:, 1:2], 0.0).then_inc(conv_done, 2)
                        V.memset(tick[:, 2:3], 0.0).then_inc(xs_done, 2)

                        def step(n, r):
                            dve.wait_ge(unit_done, 4 * r + (p.u0 + n + 1))
                            a, b = p.a0 + n, n % 2
                            w = cw[:, bass.ds(4 * r + n, 1), :].rearrange("p o k -> p (o k)")
                            dve.wait_ge(pad_done, 4 * r + (n + 1))
                            dve.wait_ge(xs_done, 4 * r + (n + 1))
                            for k in range(5):
                                src = pad[:, b, k:k + T + 4]
                                if k == 0:
                                    V.tensor_scalar(cv[:, b, :], src, w[:, 0:1], w[:, 5:6], ALU.mult, ALU.add).then_inc(acc_free, 1)
                                    dve.wait_ge(acc_free, 4 * r + (SLOTS + a + 1))
                                else:
                                    ins = V.scalar_tensor_tensor(cv[:, b, :], src, w[:, k:k + 1], cv[:, b, :], ALU.mult, ALU.add)
                                    if k < 4:
                                        ins.then_inc(conv_step, 1)
                                        dve.wait_ge(conv_step, 12 * r + (3 * n + k))
                            ins.then_inc(conv_done, 1)
                            ahead(p, n, r)
                        steps(dve, p.N, 2, step)
                    elif p.name == "sz":
                        for n in range(p.N):
                            dve.wait_ge(unit_done, p.u0 + n + 1)
                            ahead(p, n, 0)
                            dve.wait_ge(z_done, n + 1)
                            dve.wait_ge(acc_free, SLOTS + p.a0 + n)
                            V.memset(tick[:, 2:3], 0.0).then_inc(acc_free, 1)
                    elif p.name == "sdt":
                        dve.wait_ge(unit_done, p.u0 + 1)
                        low(p.next, 1, 0)
                        V.tensor_scalar(two(dtr[:, :]), acc(p.a0), dtb, None, ALU.add).then_inc(acc_free, 1)
                        ssd(p, sub)
                    else:
                        def step(n, r):
                            dve.wait_ge(unit_done, 4 * r + (p.u0 + n + 1))
                            ahead(p, n, r)
                            a = p.a0 + n
                            dst = None if p.name == "ain" else two(one(ft, n, 2 * r))
                            if p.name == "ain":
                                V.tensor_copy(two(one(pt, n, 2 * r)), acc(a)).then_inc(acc_free, 1)
                            elif p.name in ("dnA", "aout", "soutA"):
                                V.tensor_copy(dst, acc(a)).then_inc(acc_free, 1)
                            else:
                                V.tensor_tensor(dst, dst, acc(a), ALU.add).then_inc(acc_free, 1)
                            if n < p.q:
                                mod_tile(p.t0 + n, r)
                        steps(dve, p.N, 2, step)
                    if p.name == "ain":
                        attention(p, sub)
                dve.wait_ge(acc_free, SLOTS + sub["post"].a)
                gate = slice(m0 + 2 * KD, m0 + 3 * KD)
                dve.wait_ge(mod_mac, 2 * (p.t0 + p.q))
                me(V.tensor_tensor(mod[:, gate, :], mod[:, gate, :], bmod[:, gate, :], ALU.add))
                me.wait()
                me(V.scalar_tensor_tensor(gp[:, :, :], mod[:, m0 + 2 * KD:m0 + 3 * KD, :], 1.0 if j == 1 else 0.5, npost[:, s, :, :], ALU.mult, ALU.mult))
                me.wait()
                scale = norm_scale(sub["post"])

                def update(k):
                    me.wait()
                    V.tensor_tensor(x[:, k, :], x[:, k, :], ft[:, k, :], ALU.add).then_inc(x_ready, 1)

                for k in range(KD):
                    for c, t0, t1 in SIDES:
                        me(V.scalar_tensor_tensor(ft[:, k, t0:t1], ft[:, k, t0:t1], gp[:, k, c:c + 1], scale[:, t0:t1],
                                                  ALU.mult, ALU.mult))
                    update(k)
                free_scale(sub["post"])

        @block.tensor
        def _(pe):
            pe.wait_ge(in_sem, 16 * 5)
            pe.wait_ge(consts, 1)

            def norm(N):
                pe.wait_ge(acc_free, N.a + 1)
                pe.wait_ge(ssq_add, N.add0 + N.n - 1)
                for b in range(BLK):
                    ins = nc.tensor.matmul(totals(N)[:, b:b + 1], ssq[:, chunk(b)], ones[:, 0:1], start=True, stop=True)
                ins.then_inc(tot_done, 1)
                pe.wait_ge(dg_done, N.v + 1)
                nc.tensor.matmul(scale_of(N)[:, 0:512], ones[:, :], rs[:, 0:512], start=True, stop=True)
                nc.tensor.matmul(scale_of(N)[:, 512:T], ones[:, :], rs[:, 512:T], start=True, stop=True).then_inc(rb_ready, 1)

            def unit(p, n, r, rh, rl, xn=None):
                u, a = p.u0 + n, p.a0 + n
                pe.wait_ge(acc_free, 4 * r + (a + 1))
                pe.wait_ge(lo_done, 4 * r + (u + 1))
                s = u % 2
                for k in range(p.nk):
                    if xn is not None:
                        pe.wait_ge(xn_ready, xn + k + 1)
                    for w, m in ((wh, rh), (wh, rl), (wl, rh)):
                        for b in range(2):
                            ins = nc.tensor.matmul(acc(a)[:, b, :], w[:, s, k * 128:(k + 1) * 128],
                                                   m[:, k, b * C:(b + 1) * C],
                                                   start=(k == 0 and w is wh and m is rh),
                                                   stop=(k == p.nk - 1 and w is wl))
                ins.then_inc(unit_done, 1)

            units = attention_units()

            def attention(p, sub):
                pe.wait_ge(attn_in, 16 * 4)
                for f in range(5):
                    a, src = sub["va"] + f, 5 if f == 0 else 13 + f
                    pe.wait_ge(acc_free, max(a + 1, SLOTS + p.a0 + src + 1))
                    for b in range(BLK):
                        ins = nc.tensor.transpose(flat(a % SLOTS)[:, 128 * b:128 * b + 128], pt[:, src, 128 * b:128 * b + 128], ident)
                    ins.then_inc(vtr_done, 1)
                for k in range(5):
                    a = sub["qa"] + k
                    pe.wait_ge(acc_free, a + 1)
                    pe.wait_ge(hq_sq, k + 1)
                    for b in range(2):
                        ins = nc.tensor.matmul(acc(a)[:, b, :], hones, pb[:, k % 2, b * C:(b + 1) * C], start=True, stop=True)
                    ins.then_inc(hq_sum, 1)
                for k in range(5):
                    a = sub["ra"] + k
                    pe.wait_ge(acc_free, a + 1)
                    pe.wait_ge(hq_norm, k + 1)
                    nc.tensor.matmul(flat(a % SLOTS)[:, 0:LAT], rotm, pt[:, k, CTX:T], start=True, stop=True).then_inc(rot_done, 1)
                pe.wait_ge(acc_free, SLOTS + sub["ra"] + 5)
                pe.wait_ge(roped, 5)
                for g in range(len(units) + 3):
                    if g < len(units):
                        tq, half, b, tk, _, tc, _, _ = units[g]
                        rows = slice(64 * half, 64 * half + 64)
                        q = pt[rows, tq, 128 * b:128 * b + 128]
                        if g >= 2:
                            pe.wait_ge(p_done, g - 1)
                        if b:
                            nc.tensor.matmul(scores(g)[:, 0:LAT], q, pt[rows, tk, CTX:T], start=True, stop=True)
                            ins = nc.tensor.matmul(scores(g)[:, LAT:T], q, kc[rows, tc, :], start=True, stop=True)
                        else:
                            ins = nc.tensor.matmul(scores(g)[:, 0:CTX], q, pt[rows, tk, 0:CTX], start=True, stop=True)
                        ins.then_inc(qk_done, 1)
                    if 2 <= g < len(units) + 2:
                        h = g - 2
                        pe.wait_ge(pn_done, h + 1)
                        if h >= 1:
                            pe.wait_ge(ptr_done, h)
                        for j in range(BLK if units[h][2] else 1):
                            ins = nc.tensor.transpose(flat(2)[:, 128 * j:128 * j + 128], pb[:, h % 3, 128 * j:128 * j + 128], ident)
                        ins.then_inc(tr_done, 1)
                    if g >= 3:
                        h = g - 3
                        _, half, b, _, cv, _, _, _ = units[h]
                        out = P[64 * half:64 * half + 64, 6 + h % 2, 0:128]
                        pe.wait_ge(ptr_done, h + 1)
                        if h >= 2:
                            pe.wait_ge(o_done, h - 1)
                        vs = [vt[:, 1 + j, cv:cv + 64] for j in range(BLK - 1)] + [vc[:, cv:cv + 64]] if b else [vt[:, 0, cv:cv + 64]]
                        for j, v in enumerate(vs):
                            ins = nc.tensor.matmul(out, v, ptr[:, h % 2, 128 * j:128 * j + 128], start=(j == 0), stop=(j == len(vs) - 1))
                        ins.then_inc(pv_done, 1)
                pe.wait_ge(o_done, len(units))

            def ssd(p, sub):
                mm = nc.tensor.matmul
                pe.wait_ge(ssd_in, 48)
                pe.wait_ge(acc_free, SLOTS + p.a0 + 1)
                pe.wait_ge(sp_dve, 3)
                for j in range(BLK):
                    ins = nc.tensor.transpose(P[:, 7, 64 * j:64 * j + 64], dtr[0:64, chunk(j)], ident[0:64, 0:64])
                ins.then_inc(dt_tr, 1)
                pe.wait_ge(da_done, 1)
                for j in range(BLK):
                    for w in range(2):
                        mm(flat(0)[32 * w:32 * w + 32, chunk(j)], da[:, j, 32 * w:32 * w + 32], tri[:, w, :], start=True, stop=True)
                for w in range(2):
                    mm(P[:, 2, 160 * w:160 * w + 160].rearrange("p (j h) -> p j h", j=BLK), tri[:, 2 + w, :],
                       da[:, :, 32 * w:32 * w + 32], start=True, stop=True)
                mm(P[:, 3, 0:320], ones[:, :], da[:, :, :].rearrange("p j h -> p (j h)"), start=True, stop=True).then_inc(dec_sum, 1)
                pe.wait_ge(xs_done, XT + BCT + 2)
                pe.wait_ge(dec_exp, 3)
                pe.wait_ge(st_in, 32)

                def decay_sums(i, w):
                    pe.wait_ge(rb_done, 2 * i + w + 1)
                    if i:
                        pe.wait_ge(e_done, 2 * (i - 1) + w + 1)
                    for b in range(2):
                        ins = mm(P[:, 2 * w + b, :], tri[:, 2 + w, :], rb[:, w, 512 * b:512 * b + 512], start=True, stop=True)
                    ins.then_inc(seg_done, 1)

                def chunk_state(c, j, g, w):
                    n = STATES.index((c, j, g, w))
                    pe.wait_ge(xw_done, n + 1)
                    if n:
                        pe.wait_ge(s_done, n)
                    mm(P[:, 7, :], btok[:, 128 * g:128 * g + 128], xw[:, :], start=True, stop=True).then_inc(s_sum, 1)

                for c, (j, second) in enumerate(CHUNKS):
                    for k in range(5):
                        if k >= 2:
                            pe.wait_ge(prep_cp, 5 * c + k - 1)
                        elif c:
                            pe.wait_ge(s_done, sum(1 for x in STATES if x[0] < c))
                            off = 2 * GROUPS * max(0, c - 4)
                            if off:
                                pe.wait_ge(eb_done, off)
                        for q in range(4):
                            ins = nc.tensor.transpose(P[:, 6 + k % 2, 128 * q:128 * q + 128], xs[:, 4 * k + q, chunk(j)], ident)
                        ins.then_inc(prep_tr, 1)
                    pe.wait_ge(prep_cp, 5 * c + 5)
                    if not second:
                        for g in range(GROUPS):
                            chunk_state(c, j, g, 1)
                        if c == 2:
                            decay_sums(0, 0)
                            decay_sums(0, 1)
                            pe.wait_ge(s_done, 3 * GROUPS)
                        continue
                    for g in range(GROUPS):
                        ins = mm(P[:, 7, 128 * g:128 * g + 128], xs[:, XT + g, chunk(j)], xs[:, XT + 4 + g, chunk(j)], start=True, stop=True)
                    ins.then_inc(cb_done, 1)
                    pe.wait_ge(cbt_done, 2 * (c - 2))
                    for g in range(GROUPS):
                        i = ITEMS.index((c, j, g))
                        for w in range(2):
                            if j:
                                n = 2 * (i - GROUPS) + w
                                if n:
                                    pe.wait_ge(offm_done, n)
                                S = sf if w == 0 else sbw[:, j % 2, :]
                                if w and j >= 3:
                                    pe.wait_ge(sb_back[j - 3], 16)
                                for q in range(4):
                                    t = 4 * g + q
                                    mm(P[:, 5, 128 * q:128 * q + 128], S[:, 128 * t:128 * t + 128], xs[:, XT + 4 + g, chunk(j)], start=True, stop=True)
                                for h in range(GH):
                                    k = 32 * w + GH * g + h
                                    ins = mm(P[64 * (h % 2):64 * (h % 2) + 64, 6, 128 * (h // 2):128 * (h // 2) + 128],
                                             ident[0:64, k:k + 1].to_broadcast([64, 64]), rt[0:64, chunk(j)], start=True, stop=True)
                                ins.then_inc(off_done, 1)
                            if i + 1 < len(ITEMS):
                                decay_sums(i + 1, w)
                        for w in state_dirs(j, second):
                            chunk_state(c, j, g, w)
                        pe.wait_ge(xdt_done, 2 * i + 2)
                        pe.wait_ge(m_done, 2 * i + 2)
                        if i:
                            pe.wait_ge(y_done, i)
                        for h in range(GH):
                            for w in range(2):
                                ins = mm(P[64 * (h % 2):64 * (h % 2) + 64, 4, 128 * (h // 2):128 * (h // 2) + 128],
                                         xdt[:, w, 64 * h:64 * h + 64], em[:, w, 128 * h:128 * h + 128], start=(w == 0), stop=(w == 1))
                        ins.then_inc(diag_done, 1)
                pe.wait_ge(y_done, len(ITEMS))
                norm(sub["gated"])

            nh = 0
            for si, sub in enumerate(subplan):
                norm(sub["pre"])
                for p in sub["phases"]:
                    if p is sub["phases"][0]:
                        for n in range(4):
                            unit(p, n, 0, xh, xl, 8 * si if n == 0 else None)
                        with pe.Fori(1, p.N // 4) as r:
                            for n in range(4):
                                unit(p, n, r, xh, xl)
                        for n in range(p.N // 4 * 4, p.N):
                            unit(p, n, 0, xh, xl)
                        nh += p.N // 2 if p.name == "guA" else 0
                        if p.name == "ain":
                            attention(p, sub)
                    elif p.name == "guB":
                        steps(pe, p.N, 0, lambda n, r: unit(p, n, r, xh, xl))
                        nh += p.N // 2
                    elif p.name in ("aout", "sz", "sdt", "soutA", "soutB"):
                        if p.name in ("soutA", "soutB"):
                            pe.wait_ge(y_split, KD * (1 + (p.name == "soutB")))
                        rh, rl = (yh, yl) if p.name == "soutB" else (xh, xl)
                        steps(pe, p.N, 0, lambda n, r: unit(p, n, r, rh, rl))
                        if p.name == "sdt":
                            ssd(p, sub)
                    else:
                        pe.wait_ge(h_ready, nh + 1)
                        steps(pe, p.N, 0, lambda n, r: unit(p, n, r, hh, hl))
                norm(sub["post"])


def constants():
    i = np.arange(128)
    rot = np.zeros((128, 128), np.float32)
    for o in range(0, 128, 32):
        for q in range(16):
            rot[o + 16 + q, o + q] = -1.0
            rot[o + q, o + 16 + q] = 1.0
    col = np.arange(64)
    c0 = np.clip(col - 8, 0, 48)
    inside = (col[None] >= c0[:, None]) & (col[None] < c0[:, None] + 16)
    mask = np.tile(np.where(inside, 0.0, NEG), (2, 1))
    return np.concatenate([np.eye(128), (i[:, None] // 64 == i[None] // 64), rot, mask], 1).astype(np.float32)


def rotary_tables():
    t = np.arange(LAT, dtype=np.int32)
    inv = (1.0 / (np.float32(10000.0) ** (np.arange(16, dtype=np.float32) / np.float32(16)))).astype(np.float32)
    f = np.arange(128)
    pos = np.where((f[:, None] % 64) < 32, t[None] // 64, t[None] % 64).astype(np.float32)
    ang = (pos * inv[f % 16][:, None]).astype(np.float32)
    return np.stack([np.cos(ang), np.sin(ang)], 1).astype(np.float32)


def kernel(**inp):
    import concourse.bacc as bacc
    from concourse.bass_utils import run_bass_kernel_spmd as run
    subs = SUBS
    nc = bacc.Bacc("TRN2", target_bir_lowering=False, num_devices=1)
    arrays, d = {}, {}

    def put(name, a):
        a = np.ascontiguousarray(a)
        arrays[name + "_d"] = a
        d[name] = nc.dram_tensor(name + "_d", a.shape, F32, kind="ExternalInput").ap()

    I = {k: np.asarray(v) for k, v in inp.items()}

    def feat(a):
        return a.T.reshape(-1, 128, a.shape[0]).transpose(1, 0, 2)

    def units(w):
        K, N = w.shape
        return w.reshape(K // 128, 128, N // 128, 128).transpose(2, 1, 0, 3).reshape(N // 128, 128, K)

    put("x", feat(np.concatenate([I["x_prompt"][0], I["x_sample"][0]])))
    put("cond", np.repeat(np.stack([I["c_ctx"], I["c"][0]])[:, None], 128, 1))
    two = lambda a: np.repeat(a[..., None], 2, axis=-1)
    put("bmod", two(I["b_mod"].reshape(2 * MT, 128).T))
    put("npre", two(I["norm_pre"].reshape(6, KD, 128).transpose(2, 0, 1)))
    put("npost", two(I["norm_post"].reshape(6, KD, 128).transpose(2, 0, 1)))
    put("wmod", I["w_mod"].transpose(0, 2, 1).reshape(2 * MT, 128, D))
    gu = [np.stack([units(I["ffn_w_gate"][l, f]), units(I["ffn_w_up"][l, f])], 1).reshape(2 * FFT, 128, D)
          for l in range(2) for f in range(2)]
    put("wgu", np.concatenate(gu))
    KA = HALF[0] * 128
    put("wdA", np.concatenate([units(I["ffn_w_down"][l, f][:KA]) for l in range(2) for f in range(2)]))
    put("wdB", np.concatenate([units(I["ffn_w_down"][l, f][KA:]) for l in range(2) for f in range(2)]))
    a_in, a_out = I["attn_w_in"][0], I["attn_w_out"][0]
    pair = lambda a: a.reshape(2, 4, HD, -1).transpose(1, 0, 2, 3).reshape(8 * HD, -1)
    put("ain", units(np.concatenate([pair(a_in[:, :512].T).T, a_in[:, 512:]], 1)))
    put("aout", units(np.concatenate([pair(a_out[:512]), a_out[512:]])))
    put("gqk", np.stack([np.tile(I["attn_q_norm"][0], 2), np.tile(I["attn_k_norm"][0], 2)], 1))
    put("kc", np.concatenate([I["cache_attn_k"].reshape(128, 128), I["cache_na_k"].reshape(128, 512)], 1).T.reshape(5, 128, 128).transpose(1, 0, 2))
    put("vc", np.concatenate([I["cache_attn_v"].reshape(128, 128), I["cache_na_v"].reshape(128, 512)], 1))
    put("cst", constants())
    put("trig", rotary_tables())
    rpb = np.pad(I["na_rpb"][0], ((0, 0), (0, 0), (48, 48)))
    rows = np.stack([rpb[:, :, 63 - c:127 - c] for c in range(64)], 1)
    put("bias", np.concatenate([rows[:, :, 1:15], rows[:, :, 0:14]], 1).reshape(HEADS, 128, 14 * 64))
    s_in, s_out, di = I["ssd_w_in"][0], I["ssd_w_out"][0], 128 * ZT
    cdim = 128 * (XT + BCT)
    put("sz", units(s_in[:, :di]))
    put("sx", units(s_in[:, di:di + cdim]))
    put("sdt", units(np.pad(s_in[:, di + cdim:], ((0, 0), (0, 64)))))
    put("soutA", units(s_out[:D]))
    put("soutB", units(s_out[D:]))
    conv = np.concatenate([I["ssd_conv_w"][0], I["ssd_conv_b"]])
    put("cw", conv.reshape(6, XT + BCT, 128).transpose(2, 1, 0))
    per_tile = lambda a: a.reshape(XT, 128).T
    put("svec", np.concatenate([per_tile(np.repeat(I["ssd_d"][0], HD)), per_tile(I["ssd_norm"][0]),
                                np.tile(I["ssd_a_log"][0].reshape(1, 64), (128, 1)),
                                np.pad(I["ssd_dt_bias"][0], (0, 64))[:, None]], 1))
    put("s0", np.stack([I[n].reshape(2048, 128).T for n in ("state_ssd_fwd", "state_ssd_bwd")]))
    i = np.arange(128)
    a, b = i[:, None], i[None]
    put("tri", np.stack([a <= b, a >= b, a > b, a < b], 1).astype(np.float32))
    d["spill"] = nc.dram_tensor("spill_d", (128, 2048), F32).ap()
    d["zspill"] = nc.dram_tensor("zspill_d", (ZT, 128, T), F32).ap()
    d["s_ctx"] = nc.dram_tensor("s_ctx_d", (2, 128, 2048), F32, kind="ExternalOutput").ap()
    d["kv"] = nc.dram_tensor("kv_d", (128, 10, CTX), F32, kind="ExternalOutput").ap()
    d["y"] = nc.dram_tensor("y_d", (128, KD, T), F32, kind="ExternalOutput").ap()
    build(nc, d, subs)
    r = run(nc, [arrays], core_ids=[0]).results[0]
    y = r["y_d"].transpose(1, 0, 2).reshape(D, T).T
    kv = r["kv_d"].transpose(1, 0, 2).reshape(10 * 128, CTX).T
    cut = lambda a, h: a.reshape(1, 1, CTX, h, HD)
    out = (y[None, :CTX], y[None, CTX:], cut(kv[:, 0:128], 2), cut(kv[:, 128:256], 2), cut(kv[:, 256:768], 8),
           cut(kv[:, 768:1280], 8))
    return out + tuple(r["s_ctx_d"][w].T.reshape(1, 1, 32, HD, 128) for w in range(2))


SUBS = (0, 1, 2, 3, 4, 5)
```
